# Optimizing a Trainium2 kernel written in Bass

```python
import jax
import jax.numpy as jnp
from jax import lax
import numpy as np

D_MODEL = 1024
BATCH = 1
SEQ = 512
DEPTH = 1
DEC_BATCH = 8
DEC_SEQ = 8
PAST_LEN = 512
PAGE_SIZE = 128

HEAD_DIM = 64
N_HEADS = D_MODEL // HEAD_DIM
HA = N_HEADS // 2
HB = N_HEADS - HA
DK = HEAD_DIM
DV = HEAD_DIM
WA = HA * DV
WB = HB * HEAD_DIM
MIX_WIDTH = WA + WB
CHUNK_A = 64
Q_BLOCK = 128
SB_BIAS_INIT = -6.0
PEER_HEADS = 8
PEER_NKEYS = 128
PEER_N = PEER_NKEYS * PEER_NKEYS
PEER_DQ = 256
PEER_TOPK = 16
PEER_BLOCK = 256
ALPHA = (2.0 * DEPTH) ** 0.25
BETA_INIT = (8.0 * DEPTH) ** -0.25
LN_EPS = 1e-5
RMS_EPS = 1e-6
F32 = jnp.float32
SPLITS = (HA * DK, 2 * HA * DK, 2 * HA * DK + WA, 2 * HA * DK + 2 * WA, 2 * HA * DK + 2 * WA + WB, 2 * HA * DK + 2 * WA + 2 * WB)
IN_WIDTH = 2 * HA * DK + 2 * WA + 3 * WB

kernel_name = 'hymba_hgrn2_stickbreaking_peer_step'

def _layernorm(x, g, b):
    xf = x.astype(F32)
    mu = jnp.mean(xf, axis=-1, keepdims=True)
    var = jnp.mean(jnp.square(xf - mu), axis=-1, keepdims=True)
    return ((xf - mu) * lax.rsqrt(var + LN_EPS) * g.astype(F32) + b.astype(F32)).astype(x.dtype)

def _head_rmsnorm(o, g):
    of = o.astype(F32)
    of = of * lax.rsqrt(jnp.mean(of * of, axis=-1, keepdims=True) + RMS_EPS)
    return of.reshape(*o.shape[:-2], -1) * g.astype(F32)

def _hgrn2_chunked(q, logf, k, v, s0):
    B, T = q.shape[0], q.shape[1]
    C = CHUNK_A if T % CHUNK_A == 0 else T
    n = T // C

    def to_chunks(a):
        return jnp.moveaxis(a.reshape(B, n, C, *a.shape[2:]), 1, 0).astype(F32)

    causal = jnp.tril(jnp.ones((C, C), dtype=bool))

    def step(S, inp):
        qc, lfc, kc, vc = inp
        b = jnp.cumsum(lfc, axis=1)
        o_inter = jnp.einsum('bchk,bhkv->bchv', qc * jnp.exp(b), S)
        diff = b[:, :, None] - b[:, None, :]
        decay = jnp.exp(jnp.where(causal[None, :, :, None, None], diff, -jnp.inf))
        scores = jnp.einsum('bthk,btshk,bshk->bhts', qc, decay, kc)
        o_intra = jnp.einsum('bhts,bshv->bthv', scores, vc)
        b_last = b[:, -1]
        S_new = jnp.exp(b_last)[..., None] * S + jnp.einsum('bshk,bshv->bhkv', kc * jnp.exp(b_last[:, None] - b), vc)
        return S_new, o_inter + o_intra

    S_fin, o = lax.scan(step, s0.astype(F32), (to_chunks(q), to_chunks(logf), to_chunks(k), to_chunks(v)))
    o = jnp.moveaxis(o, 0, 1).reshape(B, T, v.shape[2], v.shape[3])
    return o, S_fin

def _sb_block(qb, k, v, q_pos, k_pos, bias):
    z = jnp.einsum('bhqd,bhsd->bhqs', qb.astype(F32), k) * (HEAD_DIM ** -0.5) + bias.astype(F32)[None, :, None, None]
    mask = k_pos[None, :] < q_pos[:, None]
    log_surv = jnp.where(mask, jax.nn.log_sigmoid(-z), 0.0)
    tail = lax.cumsum(log_surv, axis=3, reverse=True) - log_surv
    a = jnp.where(mask, jnp.exp(jax.nn.log_sigmoid(z) + tail), 0.0)
    return jnp.einsum('bhqs,bhsd->bhqd', a, v)

def _stick_breaking(q, k, v, q_pos, k_pos, bias):
    B, T, H, d = q.shape
    qbl = Q_BLOCK if T % Q_BLOCK == 0 else T
    nq = T // qbl
    kt = jnp.swapaxes(k, 1, 2).astype(F32)
    vt = jnp.swapaxes(v, 1, 2).astype(F32)
    q_blocks = jnp.moveaxis(jnp.swapaxes(q, 1, 2).reshape(B, H, nq, qbl, d), 2, 0)
    pos_blocks = q_pos.reshape(nq, qbl)
    o = lax.map(lambda a: _sb_block(a[0], kt, vt, a[1], k_pos, bias), (q_blocks, pos_blocks))
    return jnp.swapaxes(jnp.moveaxis(o, 0, 2).reshape(B, H, T, d), 1, 2)

def _peer(h, wq, k1, k2, u, vtab):
    shp = h.shape
    x = h.reshape(-1, shp[-1])
    T = x.shape[0]
    n = -(-T // PEER_BLOCK)
    xp = jnp.pad(x, ((0, n * PEER_BLOCK - T), (0, 0)))

    def one(xb):
        q = (xb @ wq).reshape(PEER_BLOCK, PEER_HEADS, 2, PEER_DQ // 2).astype(F32)
        s1 = jnp.einsum('thd,nd->thn', q[:, :, 0], k1.astype(F32))
        s2 = jnp.einsum('thd,nd->thn', q[:, :, 1], k2.astype(F32))
        v1, i1 = lax.top_k(s1, PEER_TOPK)
        v2, i2 = lax.top_k(s2, PEER_TOPK)
        cand = (v1[..., :, None] + v2[..., None, :]).reshape(PEER_BLOCK, PEER_HEADS, PEER_TOPK * PEER_TOPK)
        cidx = (i1[..., :, None] * PEER_NKEYS + i2[..., None, :]).reshape(PEER_BLOCK, PEER_HEADS, PEER_TOPK * PEER_TOPK)
        top_s, pos = lax.top_k(cand, PEER_TOPK)
        eidx = jnp.take_along_axis(cidx, pos, axis=-1)
        g = jax.nn.softmax(top_s, axis=-1)
        act = jax.nn.gelu(jnp.einsum('td,thkd->thk', xb, u[eidx]).astype(F32))
        return jnp.einsum('thk,thkd->td', (g * act).astype(xb.dtype), vtab[eidx])

    y = lax.map(one, xp.reshape(n, PEER_BLOCK, shp[-1]))
    return y.reshape(n * PEER_BLOCK, shp[-1])[:T].reshape(shp)

def _layer(x, c, s0, k_past, v_past, w_ada, b_ada, w_in, lb, norm_a, norm_b, sb_bias, w_out,
           ln1_g, ln1_b, ln2_g, ln2_b, peer_wq, peer_k1, peer_k2, peer_u, peer_v):
    B, T = x.shape[0], x.shape[1]
    mod = (c @ w_ada + b_ada)[:, None, :]
    sh1, sc1, g1, sh2, sc2, g2 = jnp.split(mod, 6, axis=-1)
    h = x * (1.0 + sc1) + sh1
    proj = h @ w_in
    qa, fa, ia, ga, qb, kb, vb = jnp.split(proj, list(SPLITS), axis=-1)
    z = fa.astype(F32)
    logf = jnp.log(lb + (1.0 - lb) * jax.nn.sigmoid(z))
    kin = (1.0 - lb) * jax.nn.sigmoid(-z)
    o_a, S = _hgrn2_chunked(jax.nn.silu(qa).reshape(B, T, HA, DK), logf.reshape(B, T, HA, DK),
                            kin.reshape(B, T, HA, DK), ia.reshape(B, T, HA, DV), s0)
    o_a = _head_rmsnorm(o_a, norm_a) * jax.nn.silu(ga.astype(F32))
    kb4 = kb.reshape(B, T, HB, HEAD_DIM)
    vb4 = vb.reshape(B, T, HB, HEAD_DIM)
    if k_past is None:
        past_len = 0
        k_all, v_all = kb4, vb4
    else:
        past_len = k_past.shape[1]
        k_all = jnp.concatenate([k_past.astype(kb4.dtype), kb4], axis=1)
        v_all = jnp.concatenate([v_past.astype(vb4.dtype), vb4], axis=1)
    k_pos = jnp.arange(past_len + T)
    q_pos = past_len + jnp.arange(T)
    o_b = _stick_breaking(qb.reshape(B, T, HB, HEAD_DIM), k_all, v_all, q_pos, k_pos, sb_bias)
    o_b = _head_rmsnorm(o_b, norm_b)
    mix = jnp.concatenate([o_a, o_b], axis=-1).astype(x.dtype) @ w_out
    x = _layernorm(ALPHA * x + (1.0 + g1) * mix, ln1_g, ln1_b)
    h2 = x * (1.0 + sc2) + sh2
    ff = _peer(h2, peer_wq, peer_k1, peer_k2, peer_u, peer_v)
    x = _layernorm(ALPHA * x + (1.0 + g2) * ff, ln2_g, ln2_b)
    return x, S, kb4, vb4

def _normal(k, shape, scale):
    return jax.random.normal(k, shape, F32) * scale

def setup_inputs(seed: int = 0) -> dict:
    key = jax.random.key(seed)
    ks = jax.random.split(key, 25)
    n_pages = PAST_LEN // PAGE_SIZE
    n_used = DEC_BATCH * n_pages
    n_phys = n_used + n_used // 4
    perm = jax.random.permutation(ks[0], n_phys)
    page_table = perm[:n_used].reshape(DEC_BATCH, n_pages).astype(jnp.int32)
    col_scale = jnp.concatenate([jnp.ones((2 * HA * DK,), F32), jnp.full((WA,), BETA_INIT, F32),
                                 jnp.ones((WA + 2 * WB,), F32), jnp.full((WB,), BETA_INIT, F32)])
    return {
        'x_prompt': _normal(ks[1], (BATCH, SEQ, D_MODEL), 1.0),
        'x_sample': _normal(ks[2], (DEC_BATCH, DEC_SEQ, D_MODEL), 1.0),
        'cache_k': _normal(ks[3], (DEPTH, n_phys, PAGE_SIZE, HB, HEAD_DIM), 1.0),
        'cache_v': _normal(ks[4], (DEPTH, n_phys, PAGE_SIZE, HB, HEAD_DIM), 1.0),
        'state_hgrn': _normal(ks[5], (DEPTH, DEC_BATCH, HA, DK, DV), 0.5),
        'page_table': page_table,
        'c_prompt': _normal(ks[6], (BATCH, D_MODEL), 1.0),
        'c_sample': _normal(ks[7], (DEC_BATCH, D_MODEL), 1.0),
        'w_ada': _normal(ks[8], (DEPTH, D_MODEL, 6 * D_MODEL), 0.1 * D_MODEL ** -0.5),
        'b_ada': _normal(ks[9], (DEPTH, 6 * D_MODEL), 0.02),
        'w_in': _normal(ks[10], (DEPTH, D_MODEL, IN_WIDTH), D_MODEL ** -0.5) * col_scale,
        'lb_raw': _normal(ks[11], (DEPTH + 1, HA * DK), 0.5),
        'norm_a': 1.0 + _normal(ks[12], (DEPTH, WA), 0.01),
        'norm_b': 1.0 + _normal(ks[13], (DEPTH, WB), 0.01),
        'sb_bias': SB_BIAS_INIT + _normal(ks[24], (DEPTH, HB), 0.1),
        'w_out': _normal(ks[14], (DEPTH, MIX_WIDTH, D_MODEL), BETA_INIT * MIX_WIDTH ** -0.5),
        'ln1_g': 1.0 + _normal(ks[15], (DEPTH, D_MODEL), 0.01),
        'ln1_b': _normal(ks[16], (DEPTH, D_MODEL), 0.01),
        'ln2_g': 1.0 + _normal(ks[17], (DEPTH, D_MODEL), 0.01),
        'ln2_b': _normal(ks[18], (DEPTH, D_MODEL), 0.01),
        'peer_wq': _normal(ks[19], (DEPTH, D_MODEL, PEER_HEADS * PEER_DQ), D_MODEL ** -0.5),
        'peer_k1': _normal(ks[20], (DEPTH, PEER_NKEYS, PEER_DQ // 2), (PEER_DQ // 2) ** -0.5),
        'peer_k2': _normal(ks[21], (DEPTH, PEER_NKEYS, PEER_DQ // 2), (PEER_DQ // 2) ** -0.5),
        'peer_u': _normal(ks[22], (DEPTH, PEER_N, D_MODEL), D_MODEL ** -0.5),
        'peer_v': _normal(ks[23], (DEPTH, PEER_N, D_MODEL), BETA_INIT * 0.5),
    }

def reference(x_prompt, x_sample, cache_k, cache_v, state_hgrn, page_table, c_prompt, c_sample,
              w_ada, b_ada, w_in, lb_raw, norm_a, norm_b, sb_bias, w_out, ln1_g, ln1_b, ln2_g, ln2_b,
              peer_wq, peer_k1, peer_k2, peer_u, peer_v):
    lb_all = jnp.cumsum(jax.nn.softmax(lb_raw.astype(F32), axis=0), axis=0)
    db, n_pages = page_table.shape
    page, hb, dh = cache_k.shape[2], cache_k.shape[3], cache_k.shape[4]
    past_len = n_pages * page
    yp, ys = x_prompt, x_sample
    kp_l, vp_l, sp_l, ks_l, vs_l, ss_l = [], [], [], [], [], []
    for l in range(DEPTH):
        w = (w_ada[l], b_ada[l], w_in[l], lb_all[l], norm_a[l], norm_b[l], sb_bias[l], w_out[l],
             ln1_g[l], ln1_b[l], ln2_g[l], ln2_b[l], peer_wq[l], peer_k1[l], peer_k2[l], peer_u[l], peer_v[l])
        s0 = jnp.zeros((x_prompt.shape[0], HA, DK, DV), F32)
        yp, sp, kp, vp = _layer(yp, c_prompt, s0, None, None, *w)
        k_past = cache_k[l][page_table].reshape(db, past_len, hb, dh)
        v_past = cache_v[l][page_table].reshape(db, past_len, hb, dh)
        ys, ss, ksn, vsn = _layer(ys, c_sample, state_hgrn[l], k_past, v_past, *w)
        kp_l.append(kp); vp_l.append(vp); sp_l.append(sp)
        ks_l.append(ksn); vs_l.append(vsn); ss_l.append(ss)
    k_prompt = jnp.stack(kp_l)
    v_prompt = jnp.stack(vp_l)
    s_prompt = jnp.stack(sp_l)
    k_sample = jnp.stack(ks_l)
    v_sample = jnp.stack(vs_l)
    s_sample = jnp.stack(ss_l)
    return (yp, ys, k_prompt, v_prompt, s_prompt, k_sample, v_sample, s_sample)


_drawn_inputs = setup_inputs


def setup_inputs(seed=0):
    import zlib

    import numpy as np

    out = dict(_drawn_inputs(seed))
    spreads = {}
    factors = {'norm_a': 40.323,
     'norm_b': 49.192,
     'sb_bias': 22.552,
     'ln1_g': 15.114,
     'ln1_b': 40.026,
     'ln2_g': 187.351,
     'ln2_b': 190.375,
     'cache_k': 8.0,
     'cache_v': 8.0}
    for name, (base, spread) in spreads.items():
        noise = np.random.default_rng([zlib.crc32(name.encode()), seed]).standard_normal(out[name].shape)
        drawn = base * np.exp(spread * noise) if base else spread * noise
        out[name] = jnp.asarray(drawn.astype(out[name].dtype))
    for name, factor in factors.items():
        out[name] = (out[name] * factor).astype(out[name].dtype)
    return out
```

```python
from contextlib import ExitStack

import concourse.bass as bass
from concourse import mybir

F32 = mybir.dt.float32
F32R = mybir.dt.float32r
I32 = mybir.dt.int32
U32 = mybir.dt.uint32
ALU = mybir.AluOpType
ACT = mybir.ActivationFunctionType
AX = mybir.AxisListType

P = 128
D = 1024
KC = D // P
TP = 512
SEQS, SQ = 8, 8
TS = SEQS * SQ
T = TP + TS
TT = 5
HALF = T // 2
DH = 64
HA = HB = 8
W = HA * DH
FC = W // P
PAGES = 4
NE = 128
PH = 8
TOPK = 16
SLOTS = PH * TOPK
ALPHA = 2.0 ** 0.25
LN_EPS, RMS_EPS = 1e-5, 1e-6
NSEQ = 1 + SEQS
WCOLS = 512
RING = 3
NEG = -3.0e38
SH1, SC1, G1, SH2, SC2, G2 = (KC * i for i in range(6))
QA, FA, IA, GA, QB, KB, VB = range(7)
V_BADA, V_NA, V_NB, V_L1G, V_L1B, V_L2G, V_L2B, V_LB = 0, 48, 52, 56, 64, 72, 80, 88
VROWS = 96
LEVELS = (64, 32, 16, 8, 4, 2, 1, 0)

KB_ = 1024


def rows_of(t):
    return P if t < TT - 1 else TS


class Memory:

    def __init__(self, nc):
        self.nc = nc
        self.base = nc.sbuf_base
        self.base += -self.base % 64
        self.consts = self.base
        self.X = self.consts + 13 * KB_
        self.H = self.X + 4 * KC * T
        self.O = self.H + 4 * KC * T
        self.Wr = self.O + 4 * KC * T
        self.R = self.Wr + RING * 4 * KC * WCOLS
        self.end = nc.sbuf_usable_end

    def at(self, name, offset, shape, dtype=F32):
        t = self.nc.alloc_sbuf_tensor_at(name, shape, dtype, offset=offset)
        size = 4
        for n in shape[1:]:
            size *= n
        assert offset + size <= self.end, (name, offset + size - self.end)
        return t, offset + size + -size % 32


IN_ORDER = (IA, VB, QA, FA, GA, QB, KB)


def ring_pieces():
    return ([("ada", WCOLS * i) for i in range(4)] + [("in", WCOLS * i) for i in IN_ORDER]
            + [("ada", WCOLS * i) for i in range(4, 12)] + [("out", WCOLS * i) for i in range(2)]
            + [("wq", WCOLS * i) for i in range(4)])


PIECES = ring_pieces()
N_MOD1, N_IN, N_MOD2, N_OUT, N_WQ = 0, 4, 11, 19, 21


class State:
    pass


def load_piece(eng, s, i):
    kind, col = PIECES[i]
    src = s.weights[kind][:, col:col + WCOLS].rearrange("(k p) c -> p k c", p=P)
    eng.dma_start(s.wring[:, i % RING, :, :], src).then_inc(s.w_landed[i % RING], 16)


def wait_piece(eng, s, i):
    eng.wait_ge(s.w_landed[i % RING], 16 * (i // RING + 1))


def program(nc, a, outs):
    with ExitStack() as ctx:
        s = State()
        s.sem = lambda name: ctx.enter_context(nc.semaphore(name))
        m = s.m = Memory(nc)
        s.banks = ctx.enter_context(nc.psum_tensor("banks", [P, 8, 512], F32))
        s.weights = {"ada": a["w_ada"][0], "in": a["w_in"][0], "out": a["w_out"][0], "wq": a["peer_wq"][0]}
        o = m.consts
        s.ident, o = m.at("ident", o, [P, P])
        s.ident_r, o = m.at("ident_r", o, [P, P], F32R)
        s.ones, o = m.at("ones", o, [P, P])
        s.mean_all, o = m.at("mean_all", o, [P, P])
        s.mean_head, o = m.at("mean_head", o, [P, P])
        s.modT, o = m.at("modT", o, [P, 6 * KC, NSEQ])
        s.vecT, o = m.at("vecT", o, [P, VROWS])
        s.k12T, o = m.at("k12T", o, [P, 2, NE])
        s.cT, o = m.at("cT", o, [P, KC, NSEQ])
        s.lb, o = m.at("lb", o, [P, 4, FC])
        s.sb_bias, o = m.at("sb_bias", o, [P, HB])
        s.pages, o = m.at("pages", o, [1, SEQS * PAGES], I32)
        s.same8, o = m.at("same8", o, [TS, TS])
        s.causal, o = m.at("causal", o, [P, P])
        s.tri, o = m.at("tri", o, [P, P])
        s.seqmask, o = m.at("seqmask", o, [TS, SEQS])
        s.newmask, o = m.at("newmask", o, [TS, TS])
        s.eps, o = m.at("eps", o, [P, 2])
        s.zero, o = m.at("zero", o, [P, 1])
        s.iota, o = m.at("iota", o, [P, NE])
        assert o <= m.X, o - m.X
        s.xT, _ = m.at("xT", m.X, [P, KC, T])
        s.hT, _ = m.at("hT", m.H, [P, KC, T])
        s.wring, _ = m.at("wring", m.Wr, [P, RING, KC, WCOLS])
        s.w_landed = [s.sem(f"w_landed{i}") for i in range(RING)]
        s.w_used = s.sem("w_used")
        s.stored = s.sem("stored")
        s.n_stored = 0
        vector_chain = s.sem("vector_chain")
        chained = [0]

        def link(ins):
            chained[0] += 1
            ins.then_inc(vector_chain, 1)
            nc.vector.wait_ge(vector_chain, chained[0])

        s.link = link
        s.small_in = s.sem("small_in")
        s.split = {n: s.sem(n) for n in ("w_split", "x_split", "hi_ready")}
        s.split_before = {n: 0 for n in s.split}
        s.g_stored = [s.sem(f"g_stored{i}") for i in range(2)]
        for phase in PHASES:
            phase(nc, s, a, outs)
        finish(nc, s)


def setup(nc, s, a, outs):
    m = s.m
    o = m.R
    xn, o = m.at("x_rows", o, [P, TT, D])
    cn, o = m.at("c_rows", o, [NSEQ, D])
    vr, o = m.at("vector_rows", o, [VROWS, P])
    kn, o = m.at("key_rows", o, [P, 2, P])
    ti, o = m.at("iota_t", o, [P, P], I32)
    si, o = m.at("iota_s", o, [P, P], I32)
    o = m.O
    s.levmask, o = m.at("levmask", o, [P, len(LEVELS), P], I32)
    s.reset, o = m.at("reset", o, [P, T])
    xo, o = m.at("xor", o, [P, P], I32)
    up, o = m.at("upper", o, [P, P], I32)
    ge, o = m.at("at_least", o, [P, 9, P], I32)
    x_in, c_in, v_in, k_in = (s.sem(n) for n in ("x_in", "c_in", "v_in", "k_in"))
    iotas, cleared, selected = s.sem("iotas"), s.sem("cleared"), s.sem("selected")
    turned, moved_v, moved_a = s.sem("turned"), s.sem("moved_v"), s.sem("moved_a")
    vectors = ((V_BADA, "b_ada", 48), (V_NA, "norm_a", 4), (V_NB, "norm_b", 4), (V_L1G, "ln1_g", 8),
               (V_L1B, "ln1_b", 8), (V_L2G, "ln2_g", 8), (V_L2B, "ln2_b", 8))

    with nc.Block() as block:
        @block.sync
        def _(sp):
            sp.dma_start(cn[0:1, :], a["c_prompt"]).then_inc(c_in, 16)
            sp.dma_start(cn[1:NSEQ, :], a["c_sample"]).then_inc(c_in, 16)
            load_piece(sp, s, 0)
            sp.dma_start(xn[0:TS, TT - 1, :], a["x_sample"].rearrange("b t d -> (b t) d")).then_inc(x_in, 16)
            sp.dma_start(xn[:, 0:4, :], a["x_prompt"][0].rearrange("(t p) d -> p t d", p=P)).then_inc(x_in, 16)
            for i in range(1, RING):
                load_piece(sp, s, i)

        @block.scalar
        def _(act):
            for row, name, n in vectors:
                act.dma_start(vr[row:row + n, :], a[name][0].rearrange("(r p) -> r p", p=P)).then_inc(v_in, 16)
            act.dma_start(vr[V_LB:V_LB + 8, :], a["lb_raw"].rearrange("l (r p) -> (l r) p", p=P)).then_inc(v_in, 16)
            act.dma_start(kn[:, 0, :], a["peer_k1"][0]).then_inc(k_in, 16)
            act.dma_start(kn[:, 1, :], a["peer_k2"][0]).then_inc(k_in, 16)
            act.dma_start(s.sb_bias[:, :], a["sb_bias"].broadcast_to([P, HB])).then_inc(s.small_in, 16)
            act.dma_start(s.pages[:, :], a["page_table"].rearrange("(o b) n -> o (b n)", o=1)).then_inc(s.small_in, 16)
            for g in range(1, 2 * TT, 2):
                act.wait_ge(turned, 3 + g + 1)
                n = rows_of(g // 2)
                nc.scalar.copy(s.xT[:, 4:8, (g // 2) * P:(g // 2) * P + n],
                               s.banks[:, g % 4, :].rearrange("p (k t) -> p k t", k=4)[:, :, 0:n]).then_inc(moved_a, 1)

        @block.gpsimd
        def _(pool):
            nc.gpsimd.memset(s.ident[:, :], 0.0).then_inc(cleared, 1)
            pool.wait_ge(cleared, 1)
            nc.gpsimd.affine_select(out=s.ident[:, :], in_=s.ident[:, :], compare_op=ALU.not_equal, fill=1.0,
                                    base=0, pattern=[[-1, P]], channel_multiplier=1).then_inc(selected, 1)
            nc.gpsimd.iota(ti[:, :], pattern=[[1, P]], base=0, channel_multiplier=0).then_inc(iotas, 1)
            nc.gpsimd.iota(si[:, :], pattern=[[0, P]], base=0, channel_multiplier=1).then_inc(iotas, 1)

        @block.tensor
        def _(pe):
            pe.wait_ge(selected, 1)
            pe.wait_ge(c_in, 32)
            for k in range(KC):
                last = nc.tensor.transpose(s.banks[:, 4, k * NSEQ:(k + 1) * NSEQ], cn[:, k * P:(k + 1) * P],
                                           s.ident[0:NSEQ, 0:NSEQ])
            last.then_inc(turned, 1)
            pe.wait_ge(v_in, 16 * 8)
            nc.tensor.transpose(s.banks[:, 5, 0:VROWS], vr[:, :], s.ident[0:VROWS, 0:VROWS]).then_inc(turned, 1)
            pe.wait_ge(k_in, 32)
            for i in range(2):
                last = nc.tensor.transpose(s.banks[:, 6, i * P:(i + 1) * P], kn[:, i, :], s.ident[:, :])
            last.then_inc(turned, 1)
            pe.wait_ge(x_in, 32)
            for g in range(2 * TT):
                if g >= 4:
                    pe.wait_ge(moved_a if g % 2 else moved_v, (g - 4) // 2 + 1)
                t, k0, n = g // 2, 4 * (g % 2), rows_of(g // 2)
                for k in range(4):
                    last = nc.tensor.transpose(s.banks[:, g % 4, k * P:k * P + n],
                                               xn[0:n, t, (k0 + k) * P:(k0 + k + 1) * P], s.ident[0:n, 0:n])
                last.then_inc(turned, 1)

        @block.vector
        def _(v):
            link = s.link

            nc.vector.memset(s.ones[:, :], 1.0)
            nc.vector.memset(s.mean_all[:, :], 1.0 / D)
            nc.vector.memset(s.mean_head[:, :], 0.0)
            nc.vector.memset(s.reset[:, :], 1.0)
            nc.vector.memset(s.zero[:, :], 0.0)
            nc.vector.memset(s.eps[:, 0:1], LN_EPS)
            link(nc.vector.memset(s.eps[:, 1:2], RMS_EPS))
            nc.vector.memset(s.mean_head[0:DH, 0:DH], 1.0 / DH)
            nc.vector.memset(s.mean_head[DH:P, DH:P], 1.0 / DH)
            nc.vector.memset(s.reset[:, 0:TP:P], 0.0)
            nc.vector.memset(s.reset[:, TP:T:SQ], 0.0)
            v.wait_ge(turned, 1)
            nc.vector.tensor_copy(s.cT[:, :, :], s.banks[:, 4, 0:KC * NSEQ].rearrange("p (k c) -> p k c", k=KC))
            v.wait_ge(turned, 2)
            nc.vector.tensor_copy(s.vecT[:, :], s.banks[:, 5, 0:VROWS])
            v.wait_ge(turned, 3)
            link(nc.vector.tensor_copy(s.k12T[:, :, :], s.banks[:, 6, 0:2 * P].rearrange("p (i n) -> p i n", i=2)))
            for g in range(0, 2 * TT, 2):
                v.wait_ge(turned, 3 + g + 1)
                n = rows_of(g // 2)
                nc.vector.tensor_copy(s.xT[:, 0:4, (g // 2) * P:(g // 2) * P + n],
                                      s.banks[:, g % 4, :].rearrange("p (k t) -> p k t", k=4)[:, :, 0:n]).then_inc(moved_v, 1)
            v.wait_ge(iotas, 2)
            v.wait_ge(selected, 1)
            nc.vector.tensor_copy(s.ident_r[:, :], s.ident[:, :])
            nc.vector.tensor_copy(s.iota[:, :], ti[:, :])
            nc.vector.tensor_tensor(xo[:, :], ti[:, :], si[:, :], ALU.bitwise_xor)
            nc.vector.tensor_tensor(s.causal[:, :], ti[:, :], si[:, :], ALU.is_gt)
            nc.vector.tensor_tensor(s.tri[:, :], si[:, :], ti[:, :], ALU.is_ge)
            nc.vector.tensor_scalar(s.seqmask[:, :], ti[0:TS, 0:SEQS], float(SQ), None, ALU.mult)
            link(nc.vector.tensor_tensor(up[:, :], ti[:, :], si[:, :], ALU.is_gt))
            nc.vector.tensor_scalar(s.levmask[:, len(LEVELS) - 1, :], xo[:, :], 0.0, None, ALU.is_equal)
            nc.vector.tensor_tensor(s.seqmask[:, :], si[0:TS, 0:SEQS], s.seqmask[:, :], ALU.subtract)
            nc.vector.tensor_scalar(s.newmask[:, :], xo[0:TS, 0:TS], float(SQ), None, ALU.is_lt)
            link(nc.vector.tensor_tensor(up[:, :], up[:, :], xo[:, :], ALU.mult))
            nc.vector.tensor_tensor(s.same8[:, :], s.newmask[:, :], s.tri[0:TS, 0:TS], ALU.mult)
            for i in range(8):
                last = nc.vector.tensor_scalar(ge[:, i, :], up[:, :], float(1 << i), None, ALU.is_ge)
            link(last)
            nc.vector.tensor_tensor(s.newmask[:, :], s.newmask[:, :], s.causal[0:TS, 0:TS], ALU.mult)
            nc.vector.tensor_scalar(ge[0:TS, 8, 0:SEQS], s.seqmask[:, :], 0.0, None, ALU.is_ge)
            link(nc.vector.tensor_scalar(ge[0:TS, 8, SEQS:2 * SEQS], s.seqmask[:, :], float(SQ), None, ALU.is_lt))
            nc.vector.tensor_tensor(s.seqmask[:, :], ge[0:TS, 8, 0:SEQS], ge[0:TS, 8, SEQS:2 * SEQS], ALU.mult)
            for n, half in enumerate(LEVELS[:-1]):
                i = half.bit_length() - 1
                nc.vector.tensor_tensor(s.levmask[:, n, :], ge[:, i, :], ge[:, i + 1, :], ALU.subtract)
            r0, r1 = s.vecT[:, V_LB:V_LB + 4], s.vecT[:, V_LB + 4:V_LB + 8]
            link(nc.vector.tensor_tensor(s.lb[:, 2, :], r0, r1, ALU.max))
            nc.vector.tensor_tensor(s.lb[:, 0, :], r0, s.lb[:, 2, :], ALU.subtract)
            nc.vector.tensor_tensor(s.lb[:, 1, :], r1, s.lb[:, 2, :], ALU.subtract).then_inc(s.small_in, 1)


PROJ_UNITS = []
for _piece in IN_ORDER:
    PROJ_UNITS += [(_piece, i) for i in range(TT if _piece in (IA, VB) else FC)]


FULL_UNITS = 2 * TT


def by_act(unit):
    return unit[0] in (QA, FA, GA)


def modulation_chunk(nc, s, piece, c, chunk, bank):
    for k in range(KC):
        last = nc.tensor.matmul(s.banks[:, bank, chunk * NSEQ:(chunk + 1) * NSEQ],
                                s.wring[:, piece % RING, k, c * P:(c + 1) * P], s.cT[:, k, :],
                                start=(k == 0), stop=(k == KC - 1))
    return last


def take_modulation(nc, s, bank, c0, n, plus_one):
    s.link(nc.vector.tensor_tensor(
        s.modT[:, c0:c0 + n, :], s.banks[:, bank, c0 * NSEQ:(c0 + n) * NSEQ].rearrange("p (c b) -> p c b", b=NSEQ),
        s.vecT[:, V_BADA + c0:V_BADA + c0 + n].unsqueeze(2).broadcast_to([P, n, NSEQ]), ALU.add))
    for c in plus_one:
        s.link(nc.vector.tensor_scalar(s.modT[:, c:c + KC, :], s.modT[:, c:c + KC, :], 1.0, None, ALU.add))


def project(nc, s, a, outs):
    m = s.m
    o = m.R
    s.qaT, o = m.at("qaT", o, [P, FC, T])
    s.fT, o = m.at("fT", o, [P, FC, T])
    s.kinT, o = m.at("kinT", o, [P, FC, T])
    s.ia, o = m.at("ia", o, [P, TT, W])
    s.gaT, o = m.at("gaT", o, [P, FC, T])
    s.mixfree = o
    s.qbT, o = m.at("qbT", o, [P, FC, T])
    s.kbT, o = m.at("kbT", o, [P, FC, T])
    s.vb, o = m.at("vb", o, [P, TT, W])
    s.tail = o
    mod_done, mod_moved, h_ready = s.sem("mod_done"), s.sem("mod_moved"), s.sem("h_ready")
    proj_done, took_a, took_v = s.sem("proj_done"), s.sem("took_a"), s.sem("took_v")
    lb_exp = s.sem("lb_exp")
    MODB = 6
    mod_rows, _ = m.at("mod_rows", s.tail, [NSEQ, N_IN, WCOLS])
    h_hi, _ = m.at("h_hi", s.tail, [P, KC, T], F32R)
    h_lo, _ = m.at("h_lo", m.H, [P, KC, T], F32R)
    w_hi, _ = m.at("in_hi", m.O + 4 * (len(LEVELS) * P + T), [P, 2, KC, P], F32R)
    w_lo, _ = m.at("in_lo", m.Wr, [P, RING, KC, WCOLS], F32R)
    w_split, x_split, hi_ready = (s.split[n] for n in ("w_split", "x_split", "hi_ready"))
    s.split_before = {"w_split": 2 * (len(PROJ_UNITS) - FULL_UNITS), "x_split": KC, "hi_ready": KC}
    dest = {QA: s.qaT, FA: s.fT, IA: s.ia, GA: s.gaT, QB: s.qbT, KB: s.kbT, VB: s.vb}

    with nc.Block() as block:
        @block.sync
        def _(sp):
            for i in range(RING, N_MOD2):
                sp.wait_ge(s.w_used, i - RING + 1)
                load_piece(sp, s, i)
            n = sum(not by_act(u) for u in PROJ_UNITS)
            sp.wait_ge(took_v, n)
            sp.dma_start(outs["v_prompt"].rearrange("l b (t p) h d -> p (l b t) (h d)", p=P),
                         s.vb[:, 0:4, :]).then_inc(s.stored, 16)
            sp.dma_start(outs["v_sample"].rearrange("l b t h d -> (l b t) (h d)"),
                         s.vb[0:TS, 4, :]).then_inc(s.stored, 16)
            s.n_stored += 2

        @block.tensor
        def _(pe):
            def turn_modulation(i):
                pe.wait_ge(mod_moved, i + 1)
                for c in range(4):
                    chunk = 4 * i + c
                    last = nc.tensor.transpose(s.banks[:, MODB, chunk * NSEQ:(chunk + 1) * NSEQ],
                                               mod_rows[:, i, c * P:(c + 1) * P], s.ident[0:NSEQ, 0:NSEQ])
                return last

            for i in range(N_MOD1, N_IN):
                wait_piece(pe, s, i)
                for k in range(KC):
                    last = nc.tensor.matmul(s.banks[0:NSEQ, i, :], s.cT[:, k, :], s.wring[:, i % RING, k, :],
                                            start=(k == 0), stop=(k == KC - 1))
                last.then_inc(s.w_used, 1)
                if i:
                    turn_modulation(i - 1)
            turn_modulation(N_IN - 1).then_inc(mod_done, 1)
            n_a = n_v = 0
            taken = []
            for u, unit in enumerate(PROJ_UNITS):
                piece, i = unit
                if u >= 3:
                    pe.wait_ge(*taken[u - 3])
                if i == 0:
                    wait_piece(pe, s, N_IN + IN_ORDER.index(piece))
                slot = 2 * (u % 3)
                place = (N_IN + IN_ORDER.index(piece)) % RING
                w = s.wring[:, place, :, :]
                if piece in (IA, VB):
                    n = rows_of(i)
                    for k in range(KC):
                        if u == 0:
                            pe.wait_ge(h_ready, k + 2)
                        last = nc.tensor.matmul(s.banks[0:n, slot, :], s.hT[:, k, i * P:i * P + n], w[:, k, :],
                                                start=(k == 0), stop=(k == KC - 1))
                else:
                    n = u - FULL_UNITS
                    pe.wait_ge(w_split, 2 * n + 2)
                    hi, lo = w_hi[:, n % 2, :, :], w_lo[:, place, :, i * P:(i + 1) * P]
                    for k in range(KC):
                        if n == 0:
                            pe.wait_ge(x_split, k + 1)
                        for w, x, step in ((hi, h_hi, 0), (hi, h_lo, 1), (lo, h_hi, 2)):
                            for half in range(2):
                                last = nc.tensor.matmul(s.banks[:, slot + half, 0:HALF], w[:, k, :],
                                                        x[:, k, half * HALF:(half + 1) * HALF],
                                                        start=(k == 0 and step == 0), stop=(k == KC - 1 and step == 2))
                last.then_inc(proj_done, 1)
                if i == (TT if piece in (IA, VB) else FC) - 1:
                    nc.tensor.transpose(s.banks[0:1, 7, 0:1], s.ones[0:1, 0:1], s.ident[0:1, 0:1]).then_inc(s.w_used, 1)
                if by_act(unit):
                    n_a += 1
                    taken.append((took_a, n_a))
                else:
                    n_v += 1
                    taken.append((took_v, n_v))

        @block.gpsimd
        def _(pool):
            for u in range(FULL_UNITS, len(PROJ_UNITS)):
                (piece, i), n = PROJ_UNITS[u], u - FULL_UNITS
                index = N_IN + IN_ORDER.index(piece)
                if i == 0:
                    wait_piece(pool, s, index)
                if n >= 2:
                    pool.wait_ge(proj_done, u - 1)
                columns = slice(i * P, (i + 1) * P)
                hi, w = w_hi[:, n % 2, :, :], s.wring[:, index % RING, :, columns]
                nc.gpsimd.tensor_tensor(hi, w, s.zero[:, :].unsqueeze(2).broadcast_to([P, KC, P]), ALU.add).then_inc(w_split, 1)
                pool.wait_ge(w_split, 2 * n + 1)
                nc.gpsimd.tensor_tensor(w_lo[:, index % RING, :, columns], w, hi, ALU.subtract).then_inc(w_split, 1)

        @block.scalar
        def _(act):
            act.wait_ge(s.small_in, 33)
            nc.scalar.activation(s.lb[:, 2:4, :], s.lb[:, 0:2, :], ACT.Exp).then_inc(lb_exp, 1)
            for i in range(N_MOD1, N_IN):
                act.wait_ge(s.w_used, i + 1)
                nc.scalar.copy(mod_rows[:, i, :], s.banks[0:NSEQ, i, :]).then_inc(mod_moved, 1)
            for k in range(KC):
                act.wait_ge(h_ready, k + 2)
                nc.scalar.copy(h_hi[:, k, :], s.hT[:, k, :]).then_inc(hi_ready, 1)
            for u, unit in enumerate(PROJ_UNITS):
                if not by_act(unit):
                    continue
                piece, i = unit
                act.wait_ge(proj_done, u + 1)
                src = s.banks[:, 2 * (u % 3):2 * (u % 3) + 2, 0:HALF]
                to = dest[piece][:, i, :].rearrange("p (h t) -> p h t", h=2)
                if piece == FA:
                    nc.scalar.activation(to, src, ACT.Sigmoid)
                    nc.scalar.activation(s.kinT[:, i, :].rearrange("p (h t) -> p h t", h=2), src, ACT.Sigmoid,
                                         scale=-1.0).then_inc(took_a, 1)
                else:
                    nc.scalar.activation(to, src, ACT.Silu).then_inc(took_a, 1)

        @block.vector
        def _(v):
            link = s.link

            v.wait_ge(lb_exp, 1)
            link(nc.vector.tensor_tensor(s.lb[:, 1, :], s.lb[:, 2, :], s.lb[:, 3, :], ALU.add))
            link(nc.vector.reciprocal(s.lb[:, 3, :], s.lb[:, 1, :]))
            link(nc.vector.tensor_tensor(s.lb[:, 0, :], s.lb[:, 2, :], s.lb[:, 3, :], ALU.mult))
            nc.vector.tensor_scalar(s.lb[:, 1, :], s.lb[:, 0, :], -1.0, 1.0, ALU.mult, ALU.add)

            v.wait_ge(mod_done, 1)
            take_modulation(nc, s, MODB, 0, 16, (SC1,))
            modulate(nc, s, s.xT, SC1, SH1, link, h_ready)
            for u, unit in enumerate(PROJ_UNITS):
                if u == FULL_UNITS:
                    v.wait_ge(proj_done, FULL_UNITS)
                    for k in range(KC):
                        v.wait_ge(hi_ready, k + 1)
                        nc.vector.tensor_tensor(h_lo[:, k, :], s.hT[:, k, :], h_hi[:, k, :], ALU.subtract).then_inc(x_split, 1)
                if by_act(unit):
                    continue
                piece, i = unit
                v.wait_ge(proj_done, u + 1)
                slot = 2 * (u % 3)
                if piece in (IA, VB):
                    n = rows_of(i)
                    nc.vector.tensor_copy(dest[piece][0:n, i, :], s.banks[0:n, slot, :]).then_inc(took_v, 1)
                else:
                    nc.vector.tensor_copy(dest[piece][:, i, :].rearrange("p (h t) -> p h t", h=2),
                                          s.banks[:, slot:slot + 2, 0:HALF]).then_inc(took_v, 1)


def modulate(nc, s, src, scale, shift, link, ready, after=None):
    def per_sequence(c):
        return s.modT[:, c:c + KC, 1:NSEQ].unsqueeze(3).broadcast_to([P, KC, SEQS, SQ])

    def sample(x):
        return x[:, :, TP:T].rearrange("p k (b t) -> p k b t", t=SQ)

    link(nc.vector.tensor_tensor(sample(s.hT), sample(src), per_sequence(scale), ALU.mult))
    nc.vector.tensor_tensor(sample(s.hT), sample(s.hT), per_sequence(shift), ALU.add).then_inc(ready, 1)
    for k in range(KC):
        nc.vector.tensor_scalar(s.hT[:, k, 0:TP], src[:, k, 0:TP], s.modT[:, scale + k, 0:1],
                                s.modT[:, shift + k, 0:1], ALU.mult, ALU.add).then_inc(ready, 1)
        if after is not None and k:
            after(k - 1)
    if after is not None:
        after(KC - 1)


def blocks(ap, half, n=T):
    return ap[:, 0:n].rearrange("p (b t) -> p b t", t=2 * half)


def head_rows(h):
    return slice(DH * (h % 2), DH * (h % 2) + DH)


def hgrn(nc, s, a, outs):
    m = s.m
    o = m.Wr
    bT, o = m.at("bT", o, [P, FC, T])
    qeT, o = m.at("qeT", o, [P, FC, T])
    khn, o = m.at("khn", o, [P, TT, W])
    dec, o = m.at("decay", o, [P, 2, T])
    qd, o = m.at("q_decayed", o, [P, 2, T])
    kd, o = m.at("k_decayed", o, [P, 2, T])
    assert o <= m.R
    o = s.tail
    s0, o = m.at("state_in", o, [P, FC, SEQS, DH])
    vm, o = m.at("v_of_sequence", o, [TS, 2, SEQS, DH])
    S, o = m.at("state", o, [P, FC, DH])
    Sd, o = m.at("state_decayed", o, [P, FC, DH])
    elast, o = m.at("decay_of_chunk", o, [P, FC, 4 + SEQS])
    scores, o = m.at("scores", m.H, [P, HA, TP])
    scores_s, o = m.at("scores_sample", o, [TS, HA, TS])
    s.oT, _ = m.at("oT", m.O, [P, 2 * FC, T])
    khT = s.fT
    its = [(ct, l) for ct in range(FC) for l in range(len(LEVELS))]
    DIAG = len(LEVELS) - 1
    decayed = [i for i, (_, l) in enumerate(its) if l != DIAG]
    nth = {i: n for n, i in enumerate(decayed)}
    with_sample = [LEVELS[l] <= SQ // 2 for _, l in its]

    names = ("s0_in f_ready logf_ready b_ready eb_ready kdiff_ready kexp_ready khat_ready khat_turned "
             "khn_ready diff_ready decay_ready qd_ready kd_ready scores_done scores_taken scores_clear "
             "qe_ready o_done o_taken upd_done state_ready vm_ready news_done news_taken").split()
    q = {n: s.sem("hg_" + n) for n in names}

    def scored_before(i):
        return i + 1

    with nc.Block() as block:
        @block.sync
        def _(sp):
            src = a["state_hgrn"][0].rearrange("b (c two) k v -> two c k b v", two=2)
            for par in range(2):
                for ct in range(FC):
                    sp.dma_start(s0[DH * par:DH * par + DH, ct, :, :], src[par, ct]).then_inc(q["s0_in"], 16)
            sp.wait_ge(q["state_ready"], 4)
            dst = outs["s_prompt"].rearrange("l b (c two) k v -> two k (l b c) v", two=2)
            for par in range(2):
                sp.dma_start(dst[par], S[DH * par:DH * par + DH, :, :]).then_inc(s.stored, 16)
            dst = outs["s_sample"][0].rearrange("b (c two) k v -> two c k b v", two=2)
            for ct in range(FC):
                sp.wait_ge(q["news_taken"], ct + 1)
                for par in range(2):
                    sp.dma_start(dst[par, ct], s0[DH * par:DH * par + DH, ct, :, :]).then_inc(s.stored, 16)
            s.n_stored += 2 + 2 * FC

        @block.scalar
        def _(act):
            act.wait_ge(q["f_ready"], 1)
            nc.scalar.activation(s.fT[:, :, :], s.fT[:, :, :], ACT.Ln).then_inc(q["logf_ready"], 1)
            act.wait_ge(q["b_ready"], 1)
            nc.scalar.activation(qeT[:, :, :], bT[:, :, :], ACT.Exp).then_inc(q["eb_ready"], 1)
            act.wait_ge(q["kdiff_ready"], 1)
            nc.scalar.activation(khT[:, :, :], khT[:, :, :], ACT.Exp).then_inc(q["kexp_ready"], 1)
            for n, i in enumerate(decayed):
                ct, l = its[i]
                half = LEVELS[l]
                e = blocks(dec[:, n % 2, :], half, T if with_sample[i] else TP)
                act.wait_ge(q["diff_ready"], n + 1)
                nc.scalar.activation(e[:, :, half:2 * half], e[:, :, half:2 * half], ACT.Exp)
                nc.scalar.activation(e[:, :, 0:half], e[:, :, 0:half], ACT.Exp, scale=-1.0).then_inc(q["decay_ready"], 1)
            for t in range(TT):
                act.wait_ge(q["khat_turned"], t + 1)
                n = rows_of(t)
                nc.scalar.copy(khn[0:n, t, :], s.banks[0:n, 6 + t % 2, :]).then_inc(q["khn_ready"], 1)
            for c in range(TT):
                act.wait_ge(q["o_done"], c + 1)
                n = rows_of(c)
                bank = 2 * (c % 2) if c < 4 else 2
                for par in range(2):
                    r = slice(DH * par, DH * par + DH)
                    last = nc.scalar.copy(s.oT[r, 0:FC, c * P:c * P + n],
                                          s.banks[r, bank + par, 0:FC * n].rearrange("p (c t) -> p c t", c=FC))
                last.then_inc(q["o_taken"], 1)

        @block.gpsimd
        def _(pool):
            nc.gpsimd.memset(scores_s[:, :, :], 0.0)
            nc.gpsimd.memset(scores[:, :, :], 0.0).then_inc(q["scores_clear"], 1)
            for n, i in enumerate(decayed):
                ct, l = its[i]
                cols = T if with_sample[i] else TP
                pool.wait_ge(q["decay_ready"], n + 1)
                if n >= 2:
                    pool.wait_ge(q["scores_done"], scored_before(decayed[n - 2]))
                nc.gpsimd.tensor_tensor(kd[:, n % 2, 0:cols], s.kinT[:, ct, 0:cols], dec[:, n % 2, 0:cols],
                                        ALU.mult).then_inc(q["kd_ready"], 1)

        @block.tensor
        def _(pe):
            for i, (ct, l) in enumerate(its):
                if l == DIAG:
                    qq, kk = s.qaT[:, ct, :], s.kinT[:, ct, :]
                else:
                    n = nth[i]
                    qq, kk = qd[:, n % 2, :], kd[:, n % 2, :]
                    pe.wait_ge(q["qd_ready"], n + 1)
                    pe.wait_ge(q["kd_ready"], n + 1)
                if i >= 2:
                    pe.wait_ge(q["scores_taken"], i - 1)
                slot = 2 * (i % 2)
                for par in range(2):
                    r = slice(DH * par, DH * par + DH)
                    for c in range(4):
                        last = nc.tensor.matmul(s.banks[:, slot + par, c * P:(c + 1) * P], kk[r, c * P:(c + 1) * P],
                                                qq[r, c * P:(c + 1) * P], start=True, stop=True)
                    if with_sample[i]:
                        last = nc.tensor.matmul(s.banks[0:TS, 4 + slot + par, 0:TS], kk[r, TP:T],
                                                qq[r, TP:T], start=True, stop=True)
                last.then_inc(q["scores_done"], 1)
            pe.wait_ge(q["khat_ready"], 1)
            pe.wait_ge(q["scores_taken"], len(its))
            for t in range(TT):
                n = rows_of(t)
                if t >= 2:
                    pe.wait_ge(q["khn_ready"], t - 1)
                for ct in range(FC):
                    last = nc.tensor.transpose(s.banks[0:n, 6 + t % 2, ct * P:(ct + 1) * P],
                                               khT[:, ct, t * P:t * P + n], s.ident[:, :])
                last.then_inc(q["khat_turned"], 1)
            pe.wait_ge(q["qe_ready"], 1)
            for c in range(4):
                pe.wait_ge(q["khn_ready"], c + 1)
                for ct in range(FC):
                    last = nc.tensor.matmul(s.banks[:, 4 + c % 2, ct * P:(ct + 1) * P], khn[:, c, ct * P:(ct + 1) * P],
                                            s.ia[:, c, ct * P:(ct + 1) * P], start=True, stop=True)
                last.then_inc(q["upd_done"], 1)
                if c >= 2:
                    pe.wait_ge(q["o_taken"], c - 1)
                if c:
                    pe.wait_ge(q["state_ready"], c)
                for h in range(HA):
                    r, ct = head_rows(h), h // 2
                    out = s.banks[r, 2 * (c % 2) + h % 2, ct * P:(ct + 1) * P]
                    last = nc.tensor.matmul(out, s.ia[:, c, h * DH:(h + 1) * DH], scores[:, h, c * P:(c + 1) * P],
                                            start=True, stop=(c == 0))
                    if c:
                        last = nc.tensor.matmul(out, S[r, ct, :], qeT[r, ct, c * P:(c + 1) * P], start=False, stop=True)
                last.then_inc(q["o_done"], 1)
            pe.wait_ge(q["o_taken"], 4)
            pe.wait_ge(q["s0_in"], 16 * 2 * FC)
            for h in range(HA):
                r, ct = head_rows(h), h // 2
                nc.tensor.matmul(s.banks[r, h % 2, ct * TS:(ct + 1) * TS], s.ia[0:TS, 4, h * DH:(h + 1) * DH],
                                 scores_s[:, h, :], start=True, stop=True)
                for b in range(SEQS):
                    col = ct * TS + b * SQ
                    last = nc.tensor.matmul(s.banks[r, 2 + h % 2, col:col + SQ], s0[r, ct, b, :],
                                            qeT[r, ct, TP + b * SQ:TP + (b + 1) * SQ], start=True, stop=True)
            last.then_inc(q["o_done"], 1)
            pe.wait_ge(q["khn_ready"], TT)
            pe.wait_ge(q["state_ready"], 4)
            for h in range(HA):
                r, ct = head_rows(h), h // 2
                pe.wait_ge(q["vm_ready"], h + 1)
                last = nc.tensor.matmul(s.banks[r, 4 + ct, :], khn[0:TS, 4, h * DH:(h + 1) * DH],
                                        vm[:, h % 2, :, :], start=True, stop=True)
                last.then_inc(q["news_done"], 1)

        @block.vector
        def _(v):
            link = s.link

            for ct in range(FC):
                last = nc.vector.tensor_scalar(s.fT[:, ct, :], s.fT[:, ct, :], s.lb[:, 1, ct:ct + 1],
                                               s.lb[:, 0, ct:ct + 1], ALU.mult, ALU.add)
            last.then_inc(q["f_ready"], 1)
            for ct in range(FC):
                last = nc.vector.tensor_scalar(s.kinT[:, ct, :], s.kinT[:, ct, :], s.lb[:, 1, ct:ct + 1], None, ALU.mult)
            v.wait_ge(q["logf_ready"], 1)
            for ct in range(FC):
                last = nc.vector.tensor_tensor_scan(bT[:, ct, :], s.reset[:, :], s.fT[:, ct, :], 0.0, ALU.mult, ALU.add)
            last.then_inc(q["b_ready"], 1)
            v.wait_ge(q["b_ready"], 1)
            for c0, c1, n in ((0, TP, P), (TP, T, SQ)):
                y = bT[:, :, c0:c1].rearrange("p f (c t) -> p f c t", t=n)
                last = nc.vector.tensor_tensor(khT[:, :, c0:c1].rearrange("p f (c t) -> p f c t", t=n),
                                               y[:, :, :, n - 1:n].broadcast_to([P, FC, (c1 - c0) // n, n]), y,
                                               ALU.subtract)
            last.then_inc(q["kdiff_ready"], 1)

            def diff(n):
                i = decayed[n]
                ct, l = its[i]
                half = LEVELS[l]
                cols = T if with_sample[i] else TP
                if n >= 2:
                    v.wait_ge(q["kd_ready"], n - 1)
                    v.wait_ge(q["qd_ready"], n - 1)
                b = blocks(bT[:, ct, :], half, cols)
                r = b[:, :, half - 1:half].broadcast_to([P, cols // (2 * half), 2 * half])
                nc.vector.tensor_tensor(blocks(dec[:, n % 2, :], half, cols), b, r, ALU.subtract).then_inc(q["diff_ready"], 1)

            def take(i):
                ct, l = its[i]
                v.wait_ge(q["scores_done"], i + 1)
                slot = 2 * (i % 2)
                if i:
                    v.wait_ge(q["scores_taken"], i)
                mask = s.levmask[:, l, :].unsqueeze(1).broadcast_to([P, 4, P])
                for par in range(2):
                    last = nc.vector.copy_predicated(
                        scores[:, 2 * ct + par, :].rearrange("p (c t) -> p c t", c=4), mask,
                        s.banks[:, slot + par, :].rearrange("p (c t) -> p c t", c=4))
                    if with_sample[i]:
                        last = nc.vector.copy_predicated(scores_s[:, 2 * ct + par, :], s.levmask[0:TS, l, 0:TS],
                                                         s.banks[0:TS, 4 + slot + par, 0:TS])
                last.then_inc(q["scores_taken"], 1)

            v.wait_ge(q["scores_clear"], 1)
            diff(0)
            for i, (ct, l) in enumerate(its):
                if l != DIAG:
                    n = nth[i]
                    if n + 1 < len(decayed):
                        diff(n + 1)
                    v.wait_ge(q["decay_ready"], n + 1)
                    if n >= 2:
                        v.wait_ge(q["scores_done"], scored_before(decayed[n - 2]))
                    cols = T if with_sample[i] else TP
                    nc.vector.tensor_tensor(qd[:, n % 2, 0:cols], s.qaT[:, ct, 0:cols], dec[:, n % 2, 0:cols],
                                            ALU.mult).then_inc(q["qd_ready"], 1)
                if i:
                    take(i - 1)
                if i == 0:
                    v.wait_ge(q["eb_ready"], 1)
                    nc.vector.tensor_copy(elast[:, :, 0:4], qeT[:, :, P - 1:TP:P])
                    link(nc.vector.tensor_copy(elast[:, :, 4:4 + SEQS], qeT[:, :, TP + SQ - 1:T:SQ]))
                    nc.vector.tensor_tensor(qeT[:, :, :], qeT[:, :, :], s.qaT[:, :, :], ALU.mult).then_inc(q["qe_ready"], 1)
                    v.wait_ge(q["kexp_ready"], 1)
                    nc.vector.tensor_tensor(khT[:, :, :], khT[:, :, :], s.kinT[:, :, :], ALU.mult).then_inc(q["khat_ready"], 1)
            take(len(its) - 1)
            for c in range(4):
                bank = s.banks[:, 4 + c % 2, :].rearrange("p (c x) -> p c x", c=FC)
                if c:
                    v.wait_ge(q["o_done"], c + 1)
                    link(nc.vector.tensor_tensor(Sd[:, :, :], S[:, :, :],
                                                 elast[:, :, c:c + 1].broadcast_to([P, FC, DH]), ALU.mult))
                v.wait_ge(q["upd_done"], c + 1)
                for par in range(2):
                    r = slice(DH * par, DH * par + DH)
                    own = bank[r, :, DH * par:DH * par + DH]
                    if c:
                        last = nc.vector.tensor_tensor(S[r, :, :], Sd[r, :, :], own, ALU.add)
                    else:
                        last = nc.vector.tensor_copy(S[r, :, :], own)
                last.then_inc(q["state_ready"], 1)
            for h in range(HA):
                if h >= 2:
                    v.wait_ge(q["news_done"], h - 1)
                nc.vector.tensor_tensor(vm[:, h % 2, :, :],
                                        s.ia[0:TS, 4, h * DH:(h + 1) * DH].unsqueeze(1).broadcast_to([TS, SEQS, DH]),
                                        s.seqmask[:, :].unsqueeze(2).broadcast_to([TS, SEQS, DH]),
                                        ALU.mult).then_inc(q["vm_ready"], 1)
            v.wait_ge(q["o_done"], TT)
            v.wait_ge(q["o_taken"], TT)
            for par in range(2):
                x = s.oT[DH * par:DH * par + DH, 0:FC, TP:T]
                nc.vector.tensor_tensor(x, s.banks[DH * par:DH * par + DH, par, 0:FC * TS].rearrange(
                    "p (c t) -> p c t", c=FC), x, ALU.add)
            for ct in range(FC):
                x = s0[:, ct, :, :]
                link(nc.vector.tensor_tensor(x, x, elast[:, ct, 4:4 + SEQS].unsqueeze(2).broadcast_to([P, SEQS, DH]),
                                             ALU.mult))
                v.wait_ge(q["news_done"], 2 * ct + 2)
                nc.vector.tensor_tensor(x, x, s.banks[:, 4 + ct, :].rearrange("p (b x) -> p b x", b=SEQS),
                                        ALU.add).then_inc(q["news_taken"], 1)


def head_norm(nc, s, c0, norm_row, gate, call, place):
    m = s.m
    sq, o = m.at(f"head_squares{call}", place, [P, 2, T])
    rs, o = m.at(f"head_rms{call}", o, [P, 2, T])
    if call == 0:
        s.head = [s.sem("head_" + n) for n in ("squared", "summed", "rooted", "normed")]
    squared, summed, rooted, done_sem = s.head
    before = call * FC

    def halves(ap):
        return ap.rearrange("p (h t) -> p h t", h=2)

    with nc.Block() as block:
        @block.sync
        def _(sp):
            sp.wait_ge(s.stored, 16 * s.n_stored)

        @block.tensor
        def _(pe):
            for i in range(FC):
                pe.wait_ge(squared, before + i + 1)
                if i >= 2:
                    pe.wait_ge(rooted, before + i - 1)
                for half in range(2):
                    last = nc.tensor.matmul(s.banks[:, 2 * (i % 2) + half, 0:HALF], s.mean_head[:, :],
                                            sq[:, i % 2, half * HALF:(half + 1) * HALF], start=True, stop=True)
                last.then_inc(summed, 1)

        @block.scalar
        def _(act):
            for i in range(FC):
                act.wait_ge(summed, before + i + 1)
                if i >= 2:
                    act.wait_ge(done_sem, before + i - 1)
                nc.scalar.activation(halves(rs[:, i % 2, :]), s.banks[:, 2 * (i % 2):2 * (i % 2) + 2, 0:HALF], ACT.Sqrt,
                                     bias=s.eps[:, 1:2]).then_inc(rooted, 1)

        @block.vector
        def _(v):
            link = s.link

            def square(i):
                if i >= 2:
                    v.wait_ge(summed, before + i - 1)
                x = s.oT[:, c0 + i, :]
                nc.vector.tensor_tensor(sq[:, i % 2, :], x, x, ALU.mult).then_inc(squared, 1)

            square(0)
            for i in range(FC):
                if i + 1 < FC:
                    square(i + 1)
                x, r = s.oT[:, c0 + i, :], rs[:, i % 2, :]
                v.wait_ge(rooted, before + i + 1)
                link(nc.vector.reciprocal(r, r))
                last = nc.vector.scalar_tensor_tensor(out=x, in0=x, scalar=s.vecT[:, norm_row + i:norm_row + i + 1],
                                                      in1=r, op0=ALU.mult, op1=ALU.mult)
                if gate is not None:
                    link(last)
                    last = nc.vector.tensor_tensor(x, x, gate[:, i, :], ALU.mult)
                last.then_inc(done_sem, 1)

TILE_COL = (0, 512, 1024, 896)
TILE_N = (512, 384, 256, 128)
ACOLS = 1280
PAST = SEQS * PAGES


def attention(nc, s, a, outs):
    m = s.m
    o = m.R
    zb, o = m.at("logits", o, [P, 2, ACOLS])
    sp, o = m.at("softplus", o, [P, 2, ACOLS])
    zs, _ = m.at("logits_sample", m.R, [P, TT, 512])
    ss, _ = m.at("softplus_sample", m.R + 8 * ACOLS, [P, TT, 512])
    kring, o = m.at("k_pages", o, [P, 8, W])
    kTs, o = m.at("k_pages_T", o, [P, 4, FC, P])
    assert o <= s.mixfree, (o, s.mixfree)
    vring, o = m.at("v_pages", m.H, [P, 8, W])
    assert o <= m.O
    kn, o = m.at("k_rows", s.tail, [P, TT, W])
    qblk, o = m.at("q_by_head", o, [P, FC, SEQS, 2, SQ])
    bb, o = m.at("bias_columns", o, [P, HB, SQ])
    neg, o = m.at("new_fill", o, [TS, TS])
    names = ("kv_in k_turned k_rows z_done z_taken abs_ready sp_ready sp_masked c_done d_ready "
             "d_masked a_ready o_done o_taken q_ready page_turned page_moved zs_done zs_taken ls_ready ss_ready "
             "cs_done ds_ready as_ready on_done on_taken att_act v_used mod_taken").split()
    q = {n: s.sem("at_" + n) for n in names}
    k_page = [s.sem(f"k_page{i}") for i in range(8)]
    v_page = [s.sem(f"v_page{i}") for i in range(8)]
    pages_read = s.sem("pages_read")

    def ztiles(x):
        return [x[:, c:c + n] for c, n in zip(TILE_COL, TILE_N)]

    def zbank(h, j):
        set0 = 3 * (h % 2)
        col = 384 if j == 3 else 0
        return s.banks[:, set0 + (0, 1, 2, 1)[j], col:col + TILE_N[j]]

    def pair_tokens(x, par):
        r = slice(DH * par, DH * par + DH)
        return x[r, FC:2 * FC, TP:T].rearrange("p f (b t) -> p f b t", b=SEQS)

    def pair_columns(banks, bank, par):
        r = slice(DH * par, DH * par + DH)
        return banks[r, bank, :].rearrange("p (b f x t) -> p f b x t", b=SEQS, f=FC, x=2)[:, :, :, par, :]

    with nc.Block() as block:
        @block.sync
        def _(sp_):
            for i in range(N_MOD2, N_MOD2 + RING):
                load_piece(sp_, s, i)
            sp_.wait_ge(s.small_in, 33)

            def page(cache, ring, u, landed):
                r = sp_.value_load(s.pages[0:1, u:u + 1], min_val=0, max_val=a[cache].shape[1] - 1)
                sp_.dma_start(ring[:, u % 8, :], a[cache][0, bass.ds(r, 1)].rearrange("o p h d -> (o p) (h d)")).then_inc(landed[u % 8], 16)

            for u in range(PAST):
                if u == 8:
                    for i in range(N_MOD2 + RING, N_OUT + RING):
                        sp_.wait_ge(s.w_used, i - RING + 1)
                        load_piece(sp_, s, i)
                if u >= 8:
                    sp_.wait_ge(q["page_turned"], u - 7)
                page("cache_k", kring, u, k_page)
                if u < 8:
                    page("cache_v", vring, u, v_page)
            for u in range(8, PAST):
                sp_.wait_ge(q["v_used"], (u - 8) // PAGES + 1)
                page("cache_v", vring, u, v_page)

        @block.gpsimd
        def _(pool):
            for h in range(HB):
                pool.wait_ge(q["sp_ready"], h + 1)
                for x in ztiles(sp[:, h % 2, :]):
                    last = nc.gpsimd.affine_select(out=x[:, 0:P], in_=x[:, 0:P], compare_op=ALU.is_gt, fill=0.0, base=0,
                                                   pattern=[[1, P]], channel_multiplier=-1)
                last.then_inc(q["sp_masked"], 1)
                pool.wait_ge(q["d_ready"], h + 1)
                for x in ztiles(zb[:, h % 2, :]):
                    last = nc.gpsimd.affine_select(out=x[:, 0:P], in_=x[:, 0:P], compare_op=ALU.is_gt, fill=-1.0e30, base=0,
                                                   pattern=[[1, P]], channel_multiplier=-1)
                last.then_inc(q["d_masked"], 1)

        @block.scalar
        def _(act):
            n_link = [0]

            def link(ins):
                n_link[0] += 1
                ins.then_inc(q["att_act"], 1)
                act.wait_ge(q["att_act"], n_link[0])

            for t in range(TT):
                act.wait_ge(q["k_turned"], t + 1)
                n = rows_of(t)
                nc.scalar.copy(kn[0:n, t, :], s.banks[0:n, 6 + t % 2, :]).then_inc(q["k_rows"], 1)

            act.wait_ge(q["k_rows"], TT)
            act.dma_start(outs["k_prompt"].rearrange("l b (t p) h d -> p (l b t) (h d)", p=P),
                           kn[:, 0:4, :]).then_inc(s.stored, 16)
            act.dma_start(outs["k_sample"].rearrange("l b t h d -> (l b t) (h d)"), kn[0:TS, 4, :]).then_inc(s.stored, 16)
            s.n_stored += 2

            def soft(to, z):
                link(nc.scalar.activation(to, z, ACT.Abs))
                link(nc.scalar.activation(to, to, ACT.Exp, scale=-1.0))
                return nc.scalar.activation(to, to, ACT.Ln, bias=s.ones[0:to.shape[0], 0:1])

            def front(h):
                act.wait_ge(q["z_taken"], h + 1)
                if h >= 2:
                    act.wait_ge(q["c_done"], h - 1)
                soft(sp[:, h % 2, :], zb[:, h % 2, :]).then_inc(q["abs_ready"], 1)

            def take_o(pair):
                act.wait_ge(q["o_done"], 2 * pair + 2)
                nc.scalar.copy(s.oT[:, FC + pair, 0:TP], s.banks[:, 6, :]).then_inc(q["o_taken"], 1)

            front(0)
            for h in range(HB):
                if h + 1 < HB:
                    front(h + 1)
                act.wait_ge(q["d_masked"], h + 1)
                nc.scalar.activation(zb[:, h % 2, :], zb[:, h % 2, :], ACT.Exp).then_inc(q["a_ready"], 1)
                if h >= 2 and h % 2 == 0:
                    take_o(h // 2 - 1)
            take_o(FC - 1)
            for u in range(1, PAST, 2):
                act.wait_ge(q["page_turned"], u + 1)
                if u >= 4:
                    act.wait_ge(q["zs_done"], u - 3)
                nc.scalar.copy(kTs[:, u % 4, :, :].rearrange("p f n -> p (f n)"), s.banks[:, 5 + u % 3, :]).then_inc(q["page_moved"], 1)
            act.wait_ge(q["zs_taken"], 1)
            soft(ss[:, 0:4, :], zs[:, 0:4, :])
            soft(ss[0:TS, 4, :], zs[0:TS, 4, :]).then_inc(q["ls_ready"], 1)
            act.wait_ge(q["ds_ready"], 1)
            nc.scalar.activation(zs[:, 0:4, :], zs[:, 0:4, :], ACT.Exp)
            nc.scalar.activation(zs[0:TS, 4, :], zs[0:TS, 4, :], ACT.Exp).then_inc(q["as_ready"], 1)
            act.wait_ge(q["on_done"], 1)
            for par in range(2):
                last = nc.scalar.copy(pair_tokens(s.oT, par), pair_columns(s.banks, 6, par))
            last.then_inc(q["on_taken"], 1)

        @block.tensor
        def _(pe):
            for t in range(TT):
                n = rows_of(t)
                if t >= 2:
                    pe.wait_ge(q["k_rows"], t - 1)
                for ct in range(FC):
                    last = nc.tensor.transpose(s.banks[0:n, 6 + t % 2, ct * P:(ct + 1) * P],
                                               s.kbT[:, ct, t * P:t * P + n], s.ident[:, :])
                last.then_inc(q["k_turned"], 1)

            def logits(h):
                if h >= 2:
                    pe.wait_ge(q["d_ready"], h - 1)
                r, ct = head_rows(h), h // 2
                for j in range(4):
                    last = nc.tensor.matmul(zbank(h, j), s.kbT[r, ct, j * P:(j + 1) * P], s.qbT[r, ct, j * P:TP],
                                            start=True, stop=True)
                last.then_inc(q["z_done"], 1)

            logits(0)
            for h in range(HB):
                if h + 1 < HB:
                    logits(h + 1)
                piece, chunk = N_MOD2 + h, 16 + 4 * h
                wait_piece(pe, s, piece)
                if h == 0:
                    pe.wait_ge(q["k_rows"], TT)
                for c in range(2):
                    modulation_chunk(nc, s, piece, c, chunk + c, 7)
                x = ztiles(sp[:, h % 2, :])
                pe.wait_ge(q["sp_masked"], h + 1)
                for j in range(4):
                    last = nc.tensor.matmul(zbank(h, j), s.tri[:, :], x[j], start=True, stop=(j == 3))
                    for jj in range(j + 1, 4):
                        nc.tensor.matmul(zbank(h, j)[:, (jj - j) * P:], s.ones[:, :], x[jj], start=False, stop=(jj == 3))
                last.then_inc(q["c_done"], 1)
                for c in range(2, 4):
                    last = modulation_chunk(nc, s, piece, c, chunk + c, 7)
                last.then_inc(s.w_used, 1)
                pe.wait_ge(q["a_ready"], h + 1)
                if h >= 2:
                    pe.wait_ge(q["o_taken"], h // 2)
                r = head_rows(h)
                w = ztiles(zb[:, h % 2, :])
                for j in range(4):
                    last = nc.tensor.matmul(s.banks[r, 6, j * P:TP], s.vb[:, j, h * DH:(h + 1) * DH], w[j],
                                            start=(j == 0), stop=(j == 3))
                last.then_inc(q["o_done"], 1)
            pe.wait_ge(q["o_taken"], FC)
            pe.wait_ge(q["d_ready"], HB)
            pe.wait_ge(q["q_ready"], 1)
            pe.wait_ge(q["mod_taken"], 1)

            def turn(u):
                pe.wait_ge(k_page[u % 8], 16 * (u // 8 + 1))
                if u >= 3:
                    pe.wait_ge(moved(u - 3)[0], moved(u - 3)[1])
                for ct in range(FC):
                    last = nc.tensor.transpose(s.banks[:, 5 + u % 3, ct * P:(ct + 1) * P], kring[:, u % 8, ct * P:(ct + 1) * P],
                                               s.ident[:, :])
                last.then_inc(q["page_turned"], 1)

            def moved(u):
                return (q["page_moved"], u // 2 + 1) if u % 2 else (q["kv_in"], u // 2 + 1)

            turn(0)
            for u in range(PAST):
                if u + 1 < PAST:
                    turn(u + 1)
                b, pg = u // PAGES, u % PAGES
                pe.wait_ge(*moved(u))
                for ct in range(FC):
                    col = b * TS + ct * 2 * SQ
                    last = nc.tensor.matmul(s.banks[:, pg, col:col + 2 * SQ], kTs[:, u % 4, ct, :],
                                            qblk[:, ct, b, :, :].rearrange("p x t -> p (x t)"), start=True, stop=True)
                last.then_inc(q["zs_done"], 1)
            for ct in range(FC):
                last = nc.tensor.matmul(s.banks[0:TS, 4, :].rearrange("p (b f y) -> p f b y", b=SEQS, f=FC)[:, ct],
                                        s.kbT[:, ct, TP:T], qblk[:, ct].rearrange("p b x t -> p b (x t)"), start=True, stop=True)
            last.then_inc(q["zs_done"], 1)
            pe.wait_ge(q["ss_ready"], 1)
            nc.tensor.matmul(s.banks[0:TS, 4, :], s.same8[:, :], ss[0:TS, 4, :], start=True, stop=True)
            for pg in range(PAGES):
                nc.tensor.matmul(s.banks[:, pg, :], s.tri[:, :], ss[:, pg, :], start=True, stop=False)
                for later in range(pg + 1, PAGES):
                    nc.tensor.matmul(s.banks[:, pg, :], s.ones[:, :], ss[:, later, :], start=False, stop=False)
                last = nc.tensor.matmul(s.banks[:, pg, :], s.ones[0:TS, :], ss[0:TS, 4, :], start=False, stop=True)
            last.then_inc(q["cs_done"], 1)
            pe.wait_ge(q["as_ready"], 1)
            for ct in range(FC):
                last = nc.tensor.matmul(s.banks[:, 6, :].rearrange("p (b f y) -> p f b y", b=SEQS, f=FC)[:, ct],
                                        s.vb[0:TS, 4, ct * P:(ct + 1) * P],
                                        zs[0:TS, 4, :].rearrange("p (b f y) -> p f b y", b=SEQS, f=FC)[:, ct],
                                        start=True, stop=True)
            last.then_inc(q["on_done"], 1)
            for b in range(SEQS):
                for pg in range(PAGES):
                    u = b * PAGES + pg
                    pe.wait_ge(v_page[u % 8], 16 * (u // 8 + 1))
                for ct in range(FC):
                    col = b * TS + ct * 2 * SQ
                    for pg in range(PAGES):
                        last = nc.tensor.matmul(s.banks[:, 5, col:col + 2 * SQ], vring[:, (b * PAGES + pg) % 8, ct * P:(ct + 1) * P],
                                                zs[:, pg, col:col + 2 * SQ], start=(pg == 0), stop=(pg == PAGES - 1))
                last.then_inc(q["v_used"], 1)

        @block.vector
        def _(v):
            link = s.link

            nc.vector.tensor_scalar(neg[:, :], s.newmask[:, :], -1.0, 1.0e30, ALU.add, ALU.mult)
            nc.vector.tensor_copy(bb[:, :, :], s.sb_bias[:, :].unsqueeze(2).broadcast_to([P, HB, SQ]))
            link(nc.vector.memset(qblk[:, :, :, :, :], 0.0))
            for par in range(2):
                r = slice(DH * par, DH * par + DH)
                last = nc.vector.tensor_copy(qblk[r, :, :, par, :], s.qbT[r, :, TP:T].rearrange("p f (b t) -> p f b t", b=SEQS))
            last.then_inc(q["q_ready"], 1)

            def banks_of(h):
                b = 3 * (h % 2)
                return ((s.banks[:, b:b + 2, :], lambda x: x[:, 0:1024].rearrange("p (b c) -> p b c", b=2)),
                        (s.banks[:, b + 2, 0:256], lambda x: x[:, 1024:ACOLS]))

            def take_z(h):
                v.wait_ge(q["z_done"], h + 1)
                if h >= 2:
                    v.wait_ge(q["o_done"], h - 1)
                for bank, part in banks_of(h):
                    last = nc.vector.tensor_scalar(part(zb[:, h % 2, :]), bank, DH ** -0.5, s.sb_bias[:, h:h + 1],
                                                   ALU.mult, ALU.add)
                last.then_inc(q["z_taken"], 1)

            take_z(0)
            for h in range(HB):
                if h + 1 < HB:
                    take_z(h + 1)
                v.wait_ge(q["abs_ready"], h + 1)
                x = sp[:, h % 2, :]
                nc.vector.scalar_tensor_tensor(out=x, in0=zb[:, h % 2, :], scalar=0.0, in1=x, op0=ALU.max,
                                               op1=ALU.add).then_inc(q["sp_ready"], 1)
                v.wait_ge(q["c_done"], h + 1)
                for bank, part in banks_of(h):
                    y = part(zb[:, h % 2, :])
                    last = nc.vector.tensor_tensor(y, y, bank, ALU.subtract)
                last.then_inc(q["d_ready"], 1)
            v.wait_ge(s.w_used, N_OUT)
            take_modulation(nc, s, 7, 16, 32, (G1, SC2))
            nc.vector.tensor_scalar(s.modT[:, G2:G2 + KC, :], s.modT[:, G2:G2 + KC, :], 1.0, None, ALU.add).then_inc(q["mod_taken"], 1)
            for u in range(0, PAST, 2):
                v.wait_ge(q["page_turned"], u + 1)
                if u >= 4:
                    v.wait_ge(q["zs_done"], u - 3)
                nc.vector.tensor_copy(kTs[:, u % 4, :, :].rearrange("p f n -> p (f n)"), s.banks[:, 5 + u % 3, :]).then_inc(q["kv_in"], 1)
            v.wait_ge(q["zs_done"], PAST + 1)
            v.wait_ge(q["o_done"], HB)

            def by_sequence(x):
                return x.rearrange("p (b y) -> p b y", y=TS)

            bias = bb[:, :, :].rearrange("p h t -> p (h t)").unsqueeze(1)
            nc.vector.scalar_tensor_tensor(
                out=by_sequence(zs[:, 0:4, :].rearrange("p g c -> p (g c)")), in0=by_sequence(s.banks[:, 0:4, :].rearrange("p g c -> p (g c)")),
                scalar=DH ** -0.5, in1=bias.broadcast_to([P, PAST, TS]), op0=ALU.mult, op1=ALU.add)
            nc.vector.scalar_tensor_tensor(out=by_sequence(zs[0:TS, 4, :]), in0=by_sequence(s.banks[0:TS, 4, :]), scalar=DH ** -0.5,
                                           in1=bias[0:TS].broadcast_to([TS, SEQS, TS]), op0=ALU.mult, op1=ALU.add).then_inc(q["zs_taken"], 1)
            v.wait_ge(q["ls_ready"], 1)
            nc.vector.scalar_tensor_tensor(out=ss[:, 0:4, :], in0=zs[:, 0:4, :], scalar=0.0, in1=ss[:, 0:4, :], op0=ALU.max, op1=ALU.add)
            link(nc.vector.scalar_tensor_tensor(out=ss[0:TS, 4, :], in0=zs[0:TS, 4, :], scalar=0.0, in1=ss[0:TS, 4, :],
                                                op0=ALU.max, op1=ALU.add))

            def new(x):
                return x[0:TS, 4, :].rearrange("p (b h t) -> p b h t", b=SEQS, h=HB)

            def over_heads(mask):
                return mask[:, :].rearrange("p (b t) -> p b t", b=SEQS).unsqueeze(2).broadcast_to([TS, SEQS, HB, SQ])

            nc.vector.tensor_tensor(new(ss), new(ss), over_heads(s.newmask), ALU.mult).then_inc(q["ss_ready"], 1)
            v.wait_ge(q["cs_done"], 1)
            nc.vector.tensor_tensor(zs[:, 0:4, :], zs[:, 0:4, :], s.banks[:, 0:4, :], ALU.subtract)
            link(nc.vector.tensor_tensor(zs[0:TS, 4, :], zs[0:TS, 4, :], s.banks[0:TS, 4, :], ALU.subtract))
            nc.vector.tensor_tensor(new(zs), new(zs), over_heads(neg), ALU.add).then_inc(q["ds_ready"], 1)
            v.wait_ge(q["v_used"], SEQS)
            v.wait_ge(q["on_taken"], 1)
            for par in range(2):
                x = pair_tokens(s.oT, par)
                nc.vector.tensor_tensor(x, pair_columns(s.banks, 5, par), x, ALU.add)


def halves(ap):
    return ap.rearrange("p (h t) -> p h t", h=2)


def residual(nc, v_link, s, k, gate, source, tmp, done):
    x = s.xT[:, k, :]
    for c0, c1 in ((0, HALF), (HALF, TP)):
        nc.vector.scalar_tensor_tensor(out=x[:, c0:c1], in0=source(c0, c1), scalar=s.modT[:, gate + k, 0:1],
                                       in1=x[:, c0:c1], op0=ALU.mult, op1=ALU.add)
    g = s.modT[:, gate + k, 1:NSEQ].unsqueeze(2).broadcast_to([P, SEQS, SQ])
    v_link(nc.vector.tensor_tensor(tmp[:, k % 2, :].rearrange("p (b t) -> p b t", b=SEQS),
                                   source(TP, T).rearrange("p (b t) -> p b t", b=SEQS), g, ALU.mult))
    nc.vector.tensor_tensor(x[:, TP:T], x[:, TP:T], tmp[:, k % 2, :], ALU.add).then_inc(done, 1)


def split_semaphores(s, columns):
    q = dict(s.split, before=dict(s.split_before))
    for name, n in (("w_split", 2 * columns), ("x_split", KC), ("hi_ready", KC)):
        s.split_before[name] += n
    return q


def split_weights(nc, s, pool, f, piece, parts, q):
    if f % 4 == 0:
        wait_piece(pool, s, piece)
    if f >= 2:
        pool.wait_ge(q["proj_done"], f - 1)
    hi, lo = (part[:, f % 2, :, :] for part in parts)
    w = s.wring[:, piece % RING, :, (f % 4) * P:(f % 4 + 1) * P]
    nc.gpsimd.tensor_tensor(hi, w, s.zero[:, :].unsqueeze(2).broadcast_to([P, KC, P]), ALU.add).then_inc(q["w_split"], 1)
    pool.wait_ge(q["w_split"], q["before"]["w_split"] + 2 * f + 1)
    nc.gpsimd.tensor_tensor(lo, w, hi, ALU.subtract).then_inc(q["w_split"], 1)


def split_product(nc, s, pe, f, parts, x_parts, bank, q):
    pe.wait_ge(q["w_split"], q["before"]["w_split"] + 2 * f + 2)
    hi, lo = (part[:, f % 2, :, :] for part in parts)
    x_hi, x_lo = x_parts
    for k in range(KC):
        if f == 0:
            pe.wait_ge(q["x_split"], q["before"]["x_split"] + k + 1)
        for w, x, step in ((hi, x_hi, 0), (hi, x_lo, 1), (lo, x_hi, 2)):
            for half in range(2):
                last = nc.tensor.matmul(s.banks[:, bank + half, 0:HALF], w[:, k, :], x[:, k, half * HALF:(half + 1) * HALF],
                                        start=(k == 0 and step == 0), stop=(k == KC - 1 and step == 2))
    last.then_inc(q["proj_done"], 1)


def mix_out(nc, s, a, outs):
    m = s.m
    tmp, o = m.at("gated_sample", m.R, [P, 2, TS])
    w_parts = [None, None]
    for i, name in enumerate(("out_hi", "out_lo")):
        w_parts[i], o = m.at(name, o, [P, 2, KC, P], F32R)
    o_hi, _ = m.at("o_hi", m.H, [P, KC, T], F32R)
    o_lo, _ = m.at("o_lo", m.O, [P, KC, T], F32R)
    q = split_semaphores(s, KC)
    q.update((n, s.sem("mx_" + n)) for n in ("scaled", "proj_done", "res_done"))
    scaled, proj_done, res_done = q["scaled"], q["proj_done"], q["res_done"]
    s.scaled, s.res_done = scaled, res_done

    with nc.Block() as block:
        @block.sync
        def _(sp):
            for i in range(N_OUT + RING, len(PIECES) - 1):
                sp.wait_ge(s.w_used, i - RING + 1)
                load_piece(sp, s, i)

        @block.gpsimd
        def _(pool):
            for k in range(KC):
                split_weights(nc, s, pool, k, N_OUT + k // 4, w_parts, q)

        @block.tensor
        def _(pe):
            for k in range(KC):
                if k >= 4:
                    pe.wait_ge(res_done, k - 3)
                split_product(nc, s, pe, k, w_parts, (o_hi, o_lo), 2 * (k % 4), q)

        @block.scalar
        def _(act):
            for k in range(KC):
                nc.scalar.copy(o_hi[:, k, :], s.oT[:, k, :]).then_inc(q["hi_ready"], 1)
            for k in range(KC):
                nc.scalar.mul(s.xT[:, k, :], s.xT[:, k, :], ALPHA).then_inc(scaled, 1)
            for i in range(2):
                act.wait_ge(q["w_split"], q["before"]["w_split"] + 8 * (i + 1))
                act.sem_inc(s.w_used, 1)

        @block.vector
        def _(v):
            link = s.link

            for k in range(KC):
                v.wait_ge(q["hi_ready"], q["before"]["hi_ready"] + k + 1)
                nc.vector.tensor_tensor(o_lo[:, k, :], s.oT[:, k, :], o_hi[:, k, :], ALU.subtract).then_inc(q["x_split"], 1)
            for k in range(KC):
                v.wait_ge(scaled, k + 1)
                v.wait_ge(proj_done, k + 1)
                slot = 2 * (k % 4)

                def psum(c0, c1):
                    return s.banks[:, slot + c0 // HALF, c0 % HALF:c0 % HALF + c1 - c0]

                residual(nc, link, s, k, G1, psum, tmp, res_done)


def layer_norm(nc, s, g_row, b_row, call, place):
    m = s.m
    sq, o = m.at(f"squares{call}", place, [P, 2, T])
    rstd, o = m.at(f"rstd{call}", o, [P, T])
    names = "mean_done centred squared var_done rooted normed".split()
    if call == 0:
        s.ln = {n: s.sem("ln_" + n) for n in names}
    q, once, each = s.ln, call, call * KC

    with nc.Block() as block:
        @block.tensor
        def _(pe):
            for k in range(KC):
                for half in range(2):
                    last = nc.tensor.matmul(s.banks[:, half, 0:HALF], s.mean_all[:, :],
                                            s.xT[:, k, half * HALF:(half + 1) * HALF], start=(k == 0), stop=(k == KC - 1))
            last.then_inc(q["mean_done"], 1)
            for k in range(KC):
                pe.wait_ge(q["squared"], each + k + 1)
                for half in range(2):
                    last = nc.tensor.matmul(s.banks[:, 2 + half, 0:HALF], s.mean_all[:, :],
                                            sq[:, k % 2, half * HALF:(half + 1) * HALF], start=(k == 0), stop=(k == KC - 1))
                last.then_inc(q["var_done"], 1)

        @block.scalar
        def _(act):
            for k in range(KC):
                act.wait_ge(q["centred"], each + k + 1)
                if k >= 2:
                    act.wait_ge(q["var_done"], each + k - 1)
                nc.scalar.activation(sq[:, k % 2, :], s.xT[:, k, :], ACT.Square).then_inc(q["squared"], 1)
            act.wait_ge(q["var_done"], each + KC)
            nc.scalar.activation(halves(rstd[:, :]), s.banks[:, 2:4, 0:HALF], ACT.Sqrt, bias=s.eps[:, 0:1]).then_inc(q["rooted"], 1)
            for k in range(KC):
                act.wait_ge(q["normed"], each + k + 1)
                nc.scalar.activation(s.xT[:, k, :], s.xT[:, k, :], ACT.Identity, scale=s.vecT[:, g_row + k:g_row + k + 1],
                                     bias=s.vecT[:, b_row + k:b_row + k + 1])

        @block.vector
        def _(v):
            v.wait_ge(q["mean_done"], once + 1)
            for k in range(KC):
                x = halves(s.xT[:, k, :])
                nc.vector.tensor_tensor(x, x, s.banks[:, 0:2, 0:HALF], ALU.subtract).then_inc(q["centred"], 1)
            v.wait_ge(q["rooted"], once + 1)
            s.link(nc.vector.reciprocal(rstd[:, :], rstd[:, :]))
            v.wait_ge(q["squared"], each + KC)
            for k in range(KC):
                nc.vector.tensor_tensor(s.xT[:, k, :], s.xT[:, k, :], rstd[:, :], ALU.mult).then_inc(q["normed"], 1)


NSIDE = 2 * PH
SB_STAGE = 2 * 4 * NE * TS


def query(nc, s, a, outs):
    m = s.m
    qf, o = m.at("query", m.R, [P, 4, T])
    assert o <= m.Wr + SB_STAGE
    s.sc, o = m.at("key_scores", m.Wr + SB_STAGE, [P, TT, NSIDE, NE])
    s.afterscores = o
    s.h2hi, _ = m.at("h2hi", m.O, [P, KC, T], F32R)
    s.h2lo, _ = m.at("h2lo", m.H, [P, KC, T], F32R)
    w_parts, o = [None, None], s.afterscores
    for i, name in enumerate(("wq_hi", "wq_lo")):
        w_parts[i], o = m.at(name, o, [P, 2, KC, P], F32R)
    names = "h_ready proj_done moved_v moved_a scored taken_v taken_a".split()
    q = split_semaphores(s, NSIDE)
    q.update((n, s.sem("q_" + n)) for n in names)

    def moved(f):
        return (q["moved_a"], f // 2 + 1) if f % 2 else (q["moved_v"], f // 2 + 1)

    def taken(f):
        return (q["taken_v"], f // 2 + 1) if f % 2 else (q["taken_a"], f // 2 + 1)

    def move(f, copy, eng):
        eng.wait_ge(q["proj_done"], f + 1)
        if f >= 4:
            eng.wait_ge(q["scored"], f - 3)
        slot = 2 * (f % 2)
        copy(halves(qf[:, f % 4, :]), s.banks[:, slot:slot + 2, 0:HALF]).then_inc(*((moved(f)[0], 1)))

    def take(f, copy, eng):
        eng.wait_ge(q["scored"], f + 1)
        slot = 4 + 2 * (f % 2)
        copy(s.sc[:, 0:4, f, :], s.banks[:, slot, :].rearrange("p (t n) -> p t n", t=4))
        copy(s.sc[0:TS, 4, f, :], s.banks[0:TS, slot + 1, 0:NE]).then_inc(taken(f)[0], 1)

    with nc.Block() as block:
        @block.tensor
        def _(pe):
            def score(f):
                pe.wait_ge(*moved(f))
                if f >= 2:
                    pe.wait_ge(*taken(f - 2))
                slot = 4 + 2 * (f % 2)
                for t in range(TT):
                    n = rows_of(t)
                    out = s.banks[:, slot, t * NE:(t + 1) * NE] if t < 4 else s.banks[0:TS, slot + 1, 0:NE]
                    last = nc.tensor.matmul(out, qf[:, f % 4, t * P:t * P + n], s.k12T[:, f % 2, :], start=True, stop=True)
                last.then_inc(q["scored"], 1)

            for f in range(NSIDE):
                if f >= 2:
                    pe.wait_ge(*moved(f - 2))
                split_product(nc, s, pe, f, w_parts, (s.h2hi, s.h2lo), 2 * (f % 2), q)
                if f:
                    score(f - 1)
            score(NSIDE - 1)

        @block.gpsimd
        def _(pool):
            for f in range(NSIDE):
                split_weights(nc, s, pool, f, N_WQ + f // 4, w_parts, q)

        @block.scalar
        def _(act):
            for k in range(KC):
                act.wait_ge(q["h_ready"], k + 2)
                nc.scalar.copy(s.h2hi[:, k, :], s.hT[:, k, :]).then_inc(q["hi_ready"], 1)
            for f in range(NSIDE):
                if f % 2:
                    move(f, nc.scalar.copy, act)
                else:
                    take(f, nc.scalar.copy, act)

        @block.sync
        def _(sp):
            sp.wait_ge(q["w_split"], q["before"]["w_split"] + 8)
            load_piece(sp, s, len(PIECES) - 1)

        @block.vector
        def _(v):
            link = s.link

            def lower(k):
                v.wait_ge(q["hi_ready"], q["before"]["hi_ready"] + k + 1)
                nc.vector.tensor_tensor(s.h2lo[:, k, :], s.hT[:, k, :], s.h2hi[:, k, :], ALU.subtract).then_inc(q["x_split"], 1)

            modulate(nc, s, s.xT, SC2, SH2, link, q["h_ready"], lower)
            for f in range(NSIDE):
                if f % 2 == 0:
                    move(f, nc.vector.tensor_copy, v)
                else:
                    take(f, nc.vector.tensor_copy, v)


GBLK = TS
NBLK = T // GBLK
GSUB = 4
NGRP = NE // GSUB
BODY = 8
PAIR = 2
ROWS_R, ROWS_G = 31, 17
EARLY = ROWS_R + ROWS_G
assert EARLY % BODY == 0
CREDIT = {"u_split": 3, "turned": 2, "u_parts": 1, "gelu": 2, "v_split": 4 + 1, "gated": GSUB + 1, "w_ready": 3,
          "h_stored0": 1, "h_stored1": 1}


def row_at(i, m, c):
    return i * m + c, c % 2, i * (m // 2) + c // 2


def split_u(nc, s, pool, row, raw, hi, lo):
    n, par, half = row
    q = s.q
    zero = s.zero[:, :].broadcast_to([P, D])
    pool.wait_ge(q[f"u_landed{par}"], half * 16 + 16)
    pool.wait_ge(q["turned"], n * 2 - 1 + CREDIT["turned"])
    pool.wait_ge(q["u_split"], n * 2 + CREDIT["u_split"])
    nc.gpsimd.tensor_tensor(hi[:, :], raw[:, par, :], zero, ALU.add).then_inc(q["u_split"], 1)
    pool.wait_ge(q["turned"], n * 2 + CREDIT["turned"])
    pool.wait_ge(q["u_split"], n * 2 + 1 + CREDIT["u_split"])
    nc.gpsimd.tensor_tensor(lo[:, :], raw[:, par, :], hi[:, :], ALU.subtract).then_inc(q["u_split"], 1)


def turn_u(nc, s, pe, n, part, source, bank, chunks):
    q = s.q
    if chunks[0] == 0:
        pe.wait_ge(q["u_split"], n * 2 + 1 + part + CREDIT["u_split"])
        pe.wait_ge(q["u_parts"], n * 2 + part + CREDIT["u_parts"])
    for c in chunks:
        last = nc.tensor.transpose(s.banks[:, bank + c // 4, (c % 4) * P:(c % 4 + 1) * P].bitcast(F32R),
                                   source[:, c * P:(c + 1) * P], s.ident_r[:, :])
    if chunks[-1] == KC - 1:
        last.then_inc(q["turned"], 1)


def move_u(nc, s, act, n, part, bank, target):
    act.wait_ge(s.q["turned"], n * 2 + 1 + part + CREDIT["turned"])
    nc.scalar.copy(target.rearrange("p (b c) n -> p b (c n)", b=2),
                   s.banks[:, bank:bank + 2, :].bitcast(F32R)).then_inc(s.q["u_parts"], 1)


def times_h(nc, s, pe, n, hi, lo, bank, chunks, lag=0):
    q = s.q
    if chunks[0] == 0:
        pe.wait_ge(q["u_parts"], n * 2 + 2 + CREDIT["u_parts"])
        pe.wait_ge(q["gelu"], n - lag + CREDIT["gelu"])
    for c in chunks:
        for u, h, step in ((hi, s.h2hi, 0), (hi, s.h2lo, 1), (lo, s.h2hi, 2)):
            for half in range(2):
                last = nc.tensor.matmul(s.banks[:, bank + half, 0:HALF], u[:, c, :], h[:, c, half * HALF:(half + 1) * HALF],
                                        start=(c == 0 and step == 0), stop=(c == KC - 1 and step == 2))
    if chunks[-1] == KC - 1:
        last.then_inc(q["h_done"], 1)


class Ahead:

    TURN = 4

    def __init__(self, nc, s, tag, offset, product_banks):
        o = offset
        self.banks = product_banks
        self.nc, self.s = nc, s
        self.raw, o = s.m.at("u_raw" + tag, o, [P, 2, D])
        self.rows_hi, o = s.m.at("u_rows_hi" + tag, o, [P, D], F32R)
        self.rows_lo, o = s.m.at("u_rows_lo" + tag, o, [P, D], F32R)
        self.hi, o = s.m.at("u_hi" + tag, o, [P, 2, KC, P], F32R)
        self.lo, o = s.m.at("u_lo" + tag, o, [P, 2, KC, P], F32R)
        self.out, o = s.m.at("gelu_out" + tag, o, [P, 2, T])
        assert o <= offset + 4 * TT * NSIDE * NE

    def load(self, sp, row):
        n, par, half = row
        sp.wait_ge(self.s.q["u_split"], n * 2 - 2 + CREDIT["u_split"])
        sp.dma_start(self.raw[:, par, :], self.s.u_rows[bass.ds(n, 1)].rearrange("n p d -> p (n d)")
                     ).then_inc(self.s.q[f"u_landed{par}"], 16)

    def split(self, pool, row):
        split_u(self.nc, self.s, pool, row, self.raw, self.rows_hi, self.rows_lo)

    def turn(self, pe, row, part, chunks=range(KC)):
        turn_u(self.nc, self.s, pe, row[0], part, self.rows_lo if part else self.rows_hi, self.TURN, chunks)

    def move(self, act, row, part):
        n, par, half = row
        move_u(self.nc, self.s, act, n, part, self.TURN, (self.lo if part else self.hi)[:, par, :, :])

    def product(self, pe, row, chunks=range(KC)):
        n, par, half = row
        times_h(self.nc, self.s, pe, n, self.hi[:, par, :, :], self.lo[:, par, :, :], self.banks[par], chunks,
                int(self.banks[0] != self.banks[1]))

    def gelu(self, act, row):
        n, par, half = row
        bank = self.banks[par]
        act.wait_ge(self.s.q["h_done"], n + 1)
        act.wait_ge(self.s.q[f"h_stored{par}"], half * 16 + 1)
        self.nc.scalar.activation(halves(self.out[:, par, :]), self.s.banks[:, bank:bank + 2, 0:HALF],
                                  ACT.Gelu_apprx_tanh).then_inc(self.s.q["gelu"], 1)
        act.wait_ge(self.s.q["gelu"], n + 1 + CREDIT["gelu"])
        act.dma_start(self.s.gelus[bass.ds(n, 1)].rearrange("n p t -> p (n t)"), self.out[:, par, :]
                     ).then_inc(self.s.q[f"h_stored{par}"], 16)


def retrieve(nc, s, a, outs):
    m = s.m
    o = s.afterscores
    s.slots, o = m.at("slots", o, [P, 3, T])
    cand, o = m.at("candidates", o, [P, PH, TOPK, TOPK])
    top, o = m.at("top_scores", o, [P, NSIDE, TOPK])
    ix, o = m.at("top_index", o, [P, NSIDE, TOPK], U32)
    ixf, o = m.at("top_index_f", o, [P, NSIDE, TOPK])
    best, o = m.at("best", o, [P, PH, TOPK])
    pos, o = m.at("best_position", o, [P, 3, SLOTS], U32)
    posf, o = m.at("best_parts", o, [P, 2, SLOTS])
    out3, o = m.at("rows_of_slots", o, [P, 2, 3, SLOTS])
    tot, o = m.at("weight_sum", o, [P, 2, PH])
    names = "found exp_ready rows_ready turned moved".split()
    q = {n: s.sem("r_" + n) for n in names}
    names = "u_landed0 u_landed1 u_split turned u_parts h_done gelu h_stored0 h_stored1 gated w_ready v_split y_done y_taken"
    s.q = {n: s.sem("e_" + n) for n in names.split()}
    s.u_rows = a["peer_u"][0].rearrange("(n p) d -> n p d", p=P)
    s.gelus = nc.dram_tensor("gelus", (EARLY, P, T), F32, kind="Internal").ap()
    ahead = Ahead(nc, s, "_r", m.Wr, (2, 6))
    PER_TILE = (ROWS_R - 1) // TT
    assert PER_TILE % 2 == 0 and PER_TILE * TT == ROWS_R - 1
    first, final = row_at(0, 0, 0), row_at(0, 0, ROWS_R - 1)

    with nc.Block() as block:
        @block.sync
        def _(sp):
            for name, n in CREDIT.items():
                sp.sem_inc(s.q[name], n)
            with sp.Fori(0, (ROWS_R - 1) // 2) as i:
                for c in range(2):
                    ahead.load(sp, row_at(i, 2, c))
            ahead.load(sp, final)

        @block.gpsimd
        def _(pool):
            with pool.Fori(0, (ROWS_R - 1) // 2) as i:
                for c in range(2):
                    ahead.split(pool, row_at(i, 2, c))
            ahead.split(pool, final)

        @block.scalar
        def _(act):
            def take_slots(t):
                n = rows_of(t)
                act.wait_ge(q["turned"], t + 1)
                nc.scalar.copy(s.slots[:, :, t * P:t * P + n],
                               s.banks[:, t % 2, 0:3 * P].rearrange("p (i t) -> p i t", i=3)[:, :, 0:n]).then_inc(q["moved"], 1)

            for part in range(2):
                ahead.move(act, first, part)
            for t in range(TT):
                with act.Fori(0, PER_TILE // 2) as i:
                    for c in range(2):
                        for part in range(2):
                            ahead.move(act, row_at(i, 2, PER_TILE * t + c + 1), part)
                        ahead.gelu(act, row_at(i, 2, PER_TILE * t + c))
                if t:
                    take_slots(t - 1)
                n = rows_of(t)
                act.wait_ge(q["found"], t + 1)
                w = out3[0:n, t % 2, 2, :]
                nc.scalar.activation(w, w, ACT.Exp).then_inc(q["exp_ready"], 1)
            take_slots(TT - 1)
            ahead.gelu(act, final)

        @block.tensor
        def _(pe):
            def turn_slots(t):
                n = rows_of(t)
                pe.wait_ge(q["rows_ready"], t + 1)
                if t >= 2:
                    pe.wait_ge(q["moved"], t - 1)
                for i in range(3):
                    last = nc.tensor.transpose(s.banks[:, t % 2, i * P:i * P + n], out3[0:n, t % 2, i, :], s.ident[0:n, 0:n])
                last.then_inc(q["turned"], 1)

            for part in range(2):
                ahead.turn(pe, first, part)
            for t in range(TT):
                with pe.Fori(0, PER_TILE // 2) as i:
                    for c in range(2):
                        for part in range(2):
                            ahead.turn(pe, row_at(i, 2, PER_TILE * t + c + 1), part)
                            ahead.product(pe, row_at(i, 2, PER_TILE * t + c), range(4 * part, 4 * part + 4))
                if t:
                    turn_slots(t - 1)
            turn_slots(TT - 1)
            ahead.product(pe, final)

        @block.vector
        def _(v):
            link = s.link

            def top16(n, lists, values, index):
                for r in range(2):
                    c = slice(8 * r, 8 * r + 8)
                    for x, y in zip(lists, values):
                        last = nc.vector.max(out=y[:, c], in_=x)
                    link(last)
                    for x, y, z in zip(lists, values, index):
                        last = nc.vector.max_index(out=z[:, c], in_max=y[:, c], in_values=x)
                    if r == 0:
                        for x, y in zip(lists, values):
                            last = nc.vector.match_replace(out=x, in_to_replace=y[:, c], in_values=x, imm_value=NEG)
                    link(last)

            def normalize(t):
                n = rows_of(t)
                w = out3[0:n, t % 2, 2, :].rearrange("p (h k) -> p h k", h=PH)
                v.wait_ge(q["exp_ready"], t + 1)
                link(nc.vector.tensor_reduce(tot[0:n, 0, :], w, AX.X, ALU.add))
                link(nc.vector.reciprocal(tot[0:n, 1, :], tot[0:n, 0, :]))
                nc.vector.tensor_tensor(w, w, tot[0:n, 1, :].unsqueeze(2).broadcast_to([n, PH, TOPK]), ALU.mult).then_inc(q["rows_ready"], 1)

            for t in range(TT):
                n = rows_of(t)
                sides = [s.sc[0:n, t, f, :] for f in range(NSIDE)]
                top16(n, sides, [top[0:n, f, :] for f in range(NSIDE)], [ix[0:n, f, :] for f in range(NSIDE)])
                if t:
                    normalize(t - 1)
                nc.vector.tensor_copy(ixf[0:n, :, :], ix[0:n, :, :])
                tops = top[0:n, :, :].rearrange("p (h i) k -> p h i k", i=2)
                c = cand[0:n, :, :, :]
                link(nc.vector.tensor_tensor(c, tops[:, :, 0, :].unsqueeze(3).broadcast_to([n, PH, TOPK, TOPK]),
                                             tops[:, :, 1, :].unsqueeze(2).broadcast_to([n, PH, TOPK, TOPK]), ALU.add))
                p3 = pos[0:n, :, :]
                top16(n, [cand[0:n, h, :, :].rearrange("p a b -> p (a b)") for h in range(PH)],
                      [best[0:n, h, :] for h in range(PH)],
                      [pos[0:n, 0, h * TOPK:(h + 1) * TOPK] for h in range(PH)])
                if t >= 2:
                    v.wait_ge(q["turned"], t - 1)
                o3 = out3[0:n, t % 2, :, :]
                w = o3[:, 2, :].rearrange("p (h k) -> p h k", h=PH)
                b = best[0:n, :, :]
                nc.vector.tensor_tensor(w, b, b[:, :, 0:1].broadcast_to([n, PH, TOPK]), ALU.subtract).then_inc(q["found"], 1)
                nc.vector.tensor_scalar(p3[:, 1, :], p3[:, 0, :], 4, None, ALU.logical_shift_right)
                link(nc.vector.tensor_scalar(p3[:, 2, :], p3[:, 0, :], TOPK - 1, None, ALU.bitwise_and))
                link(nc.vector.tensor_copy(posf[0:n, :, :], p3[:, 1:3, :]))
                ranks = s.iota[0:n, 0:TOPK].unsqueeze(1).broadcast_to([n, SLOTS, TOPK])
                by_side = ixf[0:n, :, :].rearrange("p (h i) k -> p h i k", i=2)
                for side in range(2):
                    eq = cand[0:n, :, :, :].rearrange("p h a b -> p (h a) b")
                    link(nc.vector.tensor_tensor(eq, posf[0:n, side, :].unsqueeze(2).broadcast_to([n, SLOTS, TOPK]), ranks, ALU.is_equal))
                    e4 = cand[0:n, :, :, :]
                    link(nc.vector.tensor_tensor(e4, e4, by_side[:, :, side, :].unsqueeze(2).broadcast_to([n, PH, TOPK, TOPK]), ALU.mult))
                    link(nc.vector.tensor_reduce(o3[:, side, :], eq, AX.X, ALU.add))
            normalize(TT - 1)


def gates(nc, s, a, outs):
    m = s.m
    stage, o = m.at("gate_stage", m.Wr, [P, 2, NE, GBLK])
    o = s.afterscores + 12 * T
    hot1, o = m.at("key1_hot", o, [P, 8, NE])
    hot2, o = m.at("key2_hot", o, [P, 8, NE])
    s.gates = nc.dram_tensor("gates", (NGRP, NE, NBLK, GSUB * GBLK), F32, kind="Internal").ap()
    names = "hot_ready done taken".split()
    q = {n: s.sem("g_" + n) for n in names}
    s.wrote_gates = [5, 4]
    GPB = GBLK // 4
    ahead = Ahead(nc, s, "_g", m.Wr + SB_STAGE, (6, 6))
    PER_BLOCK = GPB // KC
    assert PER_BLOCK * (NBLK - 1) == ROWS_G - 1
    first, final = row_at(0, 0, ROWS_R), row_at(0, 0, EARLY - 1)

    def ahead_row(i, par, g):
        return row_at(i, 2 * PER_BLOCK, ROWS_R + par * PER_BLOCK + g // KC)

    last_block = NBLK // 2

    def next_row(i, par, g):
        return row_at(i, 2 * PER_BLOCK, ROWS_R + par * PER_BLOCK + g // KC + 1)

    with nc.Block() as block:
        @block.sync
        def _(sp):
            ahead.load(sp, first)
            with sp.Fori(0, (ROWS_G - 1) // 2) as i:
                for c in range(2):
                    ahead.load(sp, row_at(i, 2, ROWS_R + 1 + c))

        @block.gpsimd
        def _(pool):
            ahead.split(pool, first)
            with pool.Fori(0, (ROWS_G - 1) // 2) as i:
                for c in range(2):
                    ahead.split(pool, row_at(i, 2, ROWS_R + 1 + c))

        @block.vector
        def _(v):
            v.sem_inc(q["done"], 2)

            def build(i, par):
                for g in range(GPB):
                    v.wait_ge(q["done"], i * (2 * GPB) + par * GPB + g + 1)
                    ring = slice((g % 2) * 4, (g % 2) * 4 + 4)
                    four = bass.ds(i * (2 * GBLK) + par * GBLK + 4 * g, 4)
                    nc.vector.tensor_tensor(hot1[:, ring, :], s.iota[:, :].unsqueeze(1).broadcast_to([P, 4, NE]),
                                            s.slots[:, 0, four].unsqueeze(2).broadcast_to([P, 4, NE]), ALU.is_equal)
                    for j in range(4):
                        at, t = (g % 2) * 4 + j, 4 * g + j
                        tok = bass.ds(i * (2 * GBLK) + par * GBLK + t, 1)
                        last = nc.vector.tensor_scalar(hot2[:, at, :], s.iota[:, :], s.slots[:, 1, tok],
                                                       s.slots[:, 2, tok], ALU.is_equal, ALU.mult)
                    last.then_inc(q["hot_ready"], 1)

            with v.Fori(0, NBLK // 2) as i:
                for par in range(2):
                    build(i, par)
            build(last_block, 0)

        @block.tensor
        def _(pe):
            def product(i, par):
                for g in range(GPB):
                    n = i * (2 * GPB) + par * GPB + g
                    pe.wait_ge(q["hot_ready"], n + 1)
                    pe.wait_ge(q["taken"], n + 1)
                    for j in range(4):
                        at = (g % 2) * 4 + j
                        last = nc.tensor.matmul(s.banks[:, g % 4, j * NE:(j + 1) * NE], hot2[:, at, :], hot1[:, at, :],
                                                start=True, stop=True)
                    last.then_inc(q["done"], 1)
                    c = g % KC
                    if i is not last_block and c in (0, 1, 4, 5):
                        ahead.turn(pe, next_row(i, par, g), c // 4, range(4 * (c % 4), 4 * (c % 4) + 4))
                    if i is not last_block or g < KC:
                        ahead.product(pe, ahead_row(i, par, g), range(c, c + 1))

            for part in range(2):
                ahead.turn(pe, first, part)
            with pe.Fori(0, NBLK // 2) as i:
                for par in range(2):
                    product(i, par)
            product(last_block, 0)

        @block.scalar
        def _(act):
            act.sem_inc(q["taken"], 4)
            for par in range(2):
                act.sem_inc(s.g_stored[par], 1)

            def take(i, par):
                act.wait_ge(s.g_stored[par], i * 16 + 1)
                for g in range(GPB):
                    act.wait_ge(q["done"], i * (2 * GPB) + par * GPB + g + 3)
                    nc.scalar.copy(stage[:, par, :, 4 * g:4 * g + 4],
                                   s.banks[:, g % 4, :].rearrange("p (j n) -> p n j", j=4)).then_inc(q["taken"], 1)
                    c = g % KC
                    if i is not last_block and c in (2, 6):
                        ahead.move(act, next_row(i, par, g), c // 4)
                    if c == KC - 1 and (i is not last_block or g < KC):
                        ahead.gelu(act, ahead_row(i, par, g))
                act.wait_ge(q["taken"], (i * 2 + par + 1) * GPB + 4)
                dst = s.gates[:, :, bass.ds(i * 2 + par, 1), :].rearrange("g p o c -> p g (o c)")
                act.dma_start(dst, stage[:, par, :, :].rearrange("p (g q) t -> p g (q t)", q=GSUB)).then_inc(s.g_stored[par], 16)

            for part in range(2):
                ahead.move(act, first, part)
            with act.Fori(0, NBLK // 2) as i:
                for par in range(2):
                    take(i, par)
            take(last_block, 0)


def experts(nc, s, a, outs):
    m = s.m
    o = m.Wr
    uraw, o = m.at("u_raw", o, [P, 2, D])
    vraw, o = m.at("v_raw", o, [P, 2, D])
    gt, o = m.at("gate_rows", o, [P, 2, NBLK, GSUB, GBLK])
    rows_hi, o = m.at("u_rows_hi", o, [P, D], F32R)
    rows_lo, o = m.at("u_rows_lo", o, [P, D], F32R)
    uhi, o = m.at("u_hi", o, [P, KC, P], F32R)
    ulo, o = m.at("u_lo", o, [P, KC, P], F32R)
    vhi, o = m.at("v_hi", o, [P, 2, PAIR, D], F32R)
    vlo, o = m.at("v_lo", o, [P, 2, PAIR, D], F32R)
    ge, o = m.at("gated", o, [P, 2, PAIR, T])
    whi, o = m.at("w_hi", o, [P, 2, PAIR, T], F32R)
    wlo, o = m.at("w_lo", o, [P, 2, PAIR, T], F32R)
    s.yT, o = m.at("yT", o, [P, KC, T])
    q = s.q
    w_hi = s.sem("w_hi")
    ge_landed = [s.sem(f"ge_landed{i}") for i in range(2)]
    v_landed = [s.sem(f"v_landed{i}") for i in range(2)]
    g_landed = [s.sem(f"g_landed{i}") for i in range(2)]
    v_rows = a["peer_v"][0].rearrange("(n p) d -> n p d", p=P)
    TURN, PROD, YBANK = 0, 2, 4
    NO_Y = 3

    def without_y(n):
        return isinstance(n, int) and n < NO_Y

    def over_rows(eng, body):
        for k in range(BODY):
            body(k, k, 0, True)
        with eng.Fori(1, EARLY // BODY) as i:
            for k in range(BODY):
                body(i * BODY + k, k, i, True)
        with eng.Fori(EARLY // BODY, NE // BODY) as i:
            for k in range(BODY):
                body(i * BODY + k, k, i, False)

    with nc.Block() as block:
        @block.sync
        def _(sp):
            for par in range(2):
                sp.wait_ge(s.g_stored[par], 16 * s.wrote_gates[par] + 1)
                sp.wait_ge(q[f"h_stored{par}"], 16 * (EARLY // 2) + 1)

            def load_v(n, k):
                sp.wait_ge(q["v_split"], n * 2 - 2 + CREDIT["v_split"])
                sp.dma_start(vraw[:, k % 2, :], v_rows[bass.ds(n, 1)].rearrange("n p d -> p (n d)")
                             ).then_inc(v_landed[k % 2], 16)

            def load(n, k, i, early):
                if without_y(n):
                    load_v(n, k)
                if k % GSUB == 0:
                    sp.wait_ge(q["gated"], n + 1)
                    sp.dma_start(gt[:, k // GSUB, :, :, :].rearrange("p b q t -> p (b q t)"),
                                 s.gates[bass.ds(i * 2 + k // GSUB, 1), :, :, :].rearrange("o p b c -> (o p) (b c)")
                                 ).then_inc(g_landed[k // GSUB], 16)
                if not early:
                    sp.wait_ge(q["u_split"], n * 2 - 2 + CREDIT["u_split"])
                    sp.dma_start(uraw[:, k % 2, :], s.u_rows[bass.ds(n, 1)].rearrange("n p d -> p (n d)")
                                 ).then_inc(q[f"u_landed{k % 2}"], 16)
                elif k % PAIR == 0:
                    g = k // PAIR
                    sp.wait_ge(q["w_ready"], n - 2 + CREDIT["w_ready"])
                    sp.dma_start(ge[:, g % 2, :, :], s.gelus[bass.ds(n, PAIR)].rearrange("n p t -> p n t")
                                 ).then_inc(ge_landed[g % 2], 16)
                if not without_y(n):
                    load_v(n, k)

            over_rows(sp, load)

        @block.gpsimd
        def _(pool):
            for par in range(2):
                pool.wait_ge(s.g_stored[par], 16 * s.wrote_gates[par] + 1)
                pool.wait_ge(q[f"h_stored{par}"], 16 * (EARLY // 2) + 1)
            zero = s.zero[:, :].broadcast_to([P, D])

            def split(n, k, i, early):
                g = (k // PAIR) % 2
                if not early:
                    split_u(nc, s, pool, (n, k % 2, i * (BODY // 2) + k // 2), uraw, rows_hi, rows_lo)
                pool.wait_ge(v_landed[k % 2], i * (16 * BODY // 2) + (k // 2 + 1) * 16)
                pool.wait_ge(q["y_done"], (n - k % PAIR) * 4 + 4)
                nc.gpsimd.tensor_tensor(vhi[:, g, k % PAIR, :], vraw[:, k % 2, :], zero, ALU.add).then_inc(q["v_split"], 1)
                pool.wait_ge(q["v_split"], n * 2 + 1 + CREDIT["v_split"])
                nc.gpsimd.tensor_tensor(vlo[:, g, k % PAIR, :], vraw[:, k % 2, :], vhi[:, g, k % PAIR, :],
                                        ALU.subtract).then_inc(q["v_split"], 1)

            over_rows(pool, split)

        @block.scalar
        def _(act):
            def row(n, k, i, early):
                g, x = (k // PAIR) % 2, k % PAIR
                if not early:
                    move_u(nc, s, act, n, 0, TURN, uhi[:, :, :])
                    move_u(nc, s, act, n, 1, TURN, ulo[:, :, :])
                    act.wait_ge(q["h_done"], n + 1)
                    act.wait_ge(q["w_ready"], n - 1 + CREDIT["w_ready"])
                    nc.scalar.activation(halves(ge[:, g, x, :]), s.banks[:, PROD:PROD + 2, 0:HALF],
                                         ACT.Gelu_apprx_tanh).then_inc(q["gelu"], 1)
                act.wait_ge(q["gated"], n + 1 + CREDIT["gated"])
                act.wait_ge(q["y_done"], (n - x) * 4 + 4)
                nc.scalar.copy(whi[:, g, x, :], ge[:, g, x, :]).then_inc(w_hi, 1)

            over_rows(act, row)

        def y_chunks(pe, n, par, chunks):
            for c in chunks:
                for x in range(PAIR):
                    bank = YBANK + 2 * (c % 2)
                    if x == 0:
                        pe.wait_ge(q["y_taken"], n + c % 2 + 1)
                    for v, w, step in ((vhi, whi, 0), (vhi, wlo, 1), (vlo, whi, 2)):
                        for half in range(2):
                            last = nc.tensor.matmul(s.banks[:, bank + half, 0:HALF], v[:, par, x, c * P:(c + 1) * P],
                                                    w[:, par, x, half * HALF:(half + 1) * HALF],
                                                    start=(x == 0 and step == 0), stop=(x == PAIR - 1 and step == 2))
                    if x == PAIR - 1:
                        last.then_inc(q["y_done"], 1)

        @block.tensor
        def _(pe):
            def row(n, k, i, early):
                odd, g = k % PAIR, (k // PAIR) % 2
                par = (g + 1) % 2 if odd else g
                if odd and not without_y(n):
                    pe.wait_ge(q["v_split"], (n - 1) * 2 + CREDIT["v_split"])
                    pe.wait_ge(q["w_ready"], n - 1 + CREDIT["w_ready"])
                for part in range(2):
                    if not early:
                        turn_u(nc, s, pe, n, part, rows_lo if part else rows_hi, TURN, range(KC))
                    c = (0 if odd else 4) + 2 * part
                    if not without_y(n):
                        y_chunks(pe, n * 4 + 2 * part, par, (c, c + 1))
                if not early:
                    times_h(nc, s, pe, n, uhi, ulo, PROD, range(KC))

            over_rows(pe, row)
            for c in (4, 6):
                y_chunks(pe, NE * 4 + c - 4, 0, (c, c + 1))
            pe.wait_ge(q["v_split"], 2 * NE + CREDIT["v_split"])
            pe.wait_ge(q["w_ready"], NE + CREDIT["w_ready"])
            for c in range(0, KC, 2):
                y_chunks(pe, NE * 4 + 4 + c, 1, (c, c + 1))

        @block.vector
        def _(v):
            for par in range(2):
                v.wait_ge(s.g_stored[par], 16 * s.wrote_gates[par] + 1)
                v.wait_ge(q[f"h_stored{par}"], 16 * (EARLY // 2) + 1)
            v.sem_inc(q["y_done"], 4 * NO_Y)
            v.sem_inc(q["y_taken"], 4 * NO_Y + 1)
            nc.vector.memset(s.yT[:, :, :], 0.0).then_inc(q["y_taken"], 1)
            v.wait_ge(q["y_taken"], 4 * NO_Y + 2)

            def add(n, c):
                v.wait_ge(q["y_done"], n + 1)
                v.wait_ge(q["y_taken"], n + 1)
                y = halves(s.yT[:, c, :])
                bank = YBANK + 2 * (c % 2)
                nc.vector.tensor_tensor(y, y, s.banks[:, bank:bank + 2, 0:HALF], ALU.add).then_inc(q["y_taken"], 1)

            def row(n, k, i, early):
                g, x = (k // PAIR) % 2, k % PAIR
                product = ge[:, g, x, :]

                def gate():
                    if not early:
                        v.wait_ge(q["gelu"], n + 1 + CREDIT["gelu"])
                    elif x == 0:
                        v.wait_ge(ge_landed[g], i * (16 * BODY // 4) + (k // 4 + 1) * 16)
                    if k % GSUB == 0:
                        v.wait_ge(g_landed[k // GSUB], i * 16 + 16)
                    by_block = product.rearrange("p (b t) -> p b t", b=NBLK)
                    nc.vector.tensor_tensor(by_block, by_block, gt[:, k // GSUB, :, k % GSUB, :],
                                            ALU.mult).then_inc(q["gated"], 1)

                for c in range(4):
                    if not without_y(n):
                        add(n * 4 + c, (0 if x else 4) + c)
                    if c == (0 if early else 3):
                        gate()
                v.wait_ge(w_hi, n + 1)
                nc.vector.tensor_tensor(wlo[:, g, x, :], product, whi[:, g, x, :], ALU.subtract).then_inc(q["w_ready"], 1)

            over_rows(v, row)
            for c in range(12):
                add(4 * NE + c, (4 + c) % KC)


def finish_y(nc, s, a, outs):
    m = s.m
    tmp, o = m.at("gated_sample2", m.H, [P, 2, TS])
    scaled, res_done = s.scaled, s.res_done
    with nc.Block() as block:
        @block.scalar
        def _(act):
            for k in range(KC):
                nc.scalar.mul(s.xT[:, k, :], s.xT[:, k, :], ALPHA).then_inc(scaled, 1)

        @block.vector
        def _(v):
            link = s.link

            for k in range(KC):
                v.wait_ge(scaled, KC + k + 1)
                residual(nc, link, s, k, G2, lambda c0, c1: s.yT[:, k, c0:c1], tmp, res_done)


def store_y(nc, s, a, outs):
    m = s.m
    rows, o = m.at("y_rows", m.Wr, [P, TT, D])
    turned, moved_v, moved_a = (s.sem("s_" + n) for n in ("turned", "moved_v", "moved_a"))
    dst_p = outs["y_prompt"][0].rearrange("(t p) d -> t p d", p=P)
    dst_s = outs["y_sample"].rearrange("b t d -> (b t) d")

    with nc.Block() as block:
        @block.tensor
        def _(pe):
            for g in range(2 * TT):
                t, k0, n = g // 2, 4 * (g % 2), rows_of(g // 2)
                if g >= 4:
                    pe.wait_ge(moved_a if g % 2 else moved_v, (g - 4) // 2 + 1)
                for k in range(4):
                    last = nc.tensor.transpose(s.banks[0:n, g % 4, k * P:(k + 1) * P], s.xT[:, k0 + k, t * P:t * P + n],
                                               s.ident[:, :])
                last.then_inc(turned, 1)

        @block.scalar
        def _(act):
            for g in range(1, 2 * TT, 2):
                act.wait_ge(turned, g + 1)
                n = rows_of(g // 2)
                nc.scalar.copy(rows[0:n, g // 2, 512:D], s.banks[0:n, g % 4, :]).then_inc(moved_a, 1)

        @block.vector
        def _(v):
            for g in range(0, 2 * TT, 2):
                v.wait_ge(turned, g + 1)
                n = rows_of(g // 2)
                nc.vector.tensor_copy(rows[0:n, g // 2, 0:512], s.banks[0:n, g % 4, :]).then_inc(moved_v, 1)

        @block.sync
        def _(sp):
            for t in range(TT):
                sp.wait_ge(moved_v, t + 1)
                sp.wait_ge(moved_a, t + 1)
                n = rows_of(t)
                sp.dma_start(dst_p[t] if t < 4 else dst_s, rows[0:n, t, :]).then_inc(s.stored, 16)
            s.n_stored += TT


PHASES = (
    setup,
    project,
    hgrn,
    lambda nc, s, a, outs: head_norm(nc, s, 0, V_NA, s.gaT, 0, s.m.H),
    attention,
    lambda nc, s, a, outs: head_norm(nc, s, FC, V_NB, None, 1, s.m.H),
    mix_out,
    lambda nc, s, a, outs: layer_norm(nc, s, V_L1G, V_L1B, 0, s.m.R),
    query,
    retrieve,
    gates,
    experts,
    finish_y,
    lambda nc, s, a, outs: layer_norm(nc, s, V_L2G, V_L2B, 1, s.m.H),
    store_y,
)


def finish(nc, s):
    with nc.Block() as block:
        @block.sync
        def _(sp):
            sp.wait_ge(s.stored, 16 * s.n_stored)


INPUTS = ("x_prompt", "x_sample", "cache_k", "cache_v", "state_hgrn", "page_table", "c_prompt", "c_sample", "w_ada",
          "b_ada", "w_in", "lb_raw", "norm_a", "norm_b", "sb_bias", "w_out", "ln1_g", "ln1_b", "ln2_g", "ln2_b",
          "peer_wq", "peer_k1", "peer_k2", "peer_u", "peer_v")
OUTPUTS = (("y_prompt", (1, TP, D)), ("y_sample", (SEQS, SQ, D)), ("k_prompt", (1, 1, TP, HB, DH)),
           ("v_prompt", (1, 1, TP, HB, DH)), ("s_prompt", (1, 1, HA, DH, DH)), ("k_sample", (1, SEQS, SQ, HB, DH)),
           ("v_sample", (1, SEQS, SQ, HB, DH)), ("s_sample", (1, SEQS, HA, DH, DH)))


def kernel(**inputs):
    import numpy as np
    import concourse.bacc as bacc
    from concourse.bass_utils import run_bass_kernel_spmd

    nc = bacc.Bacc("TRN2", target_bir_lowering=False, num_devices=1)
    arrays, a, outs = {}, {}, {}
    for name in INPUTS:
        x = np.ascontiguousarray(inputs[name])
        arrays[f"in_{name}"] = x
        a[name] = nc.dram_tensor(f"in_{name}", x.shape, mybir.dt.from_np(x.dtype), kind="ExternalInput").ap()
    for name, shape in OUTPUTS:
        outs[name] = nc.dram_tensor(f"out_{name}", shape, F32, kind="ExternalOutput").ap()
    program(nc, a, outs)
    r = run_bass_kernel_spmd(nc, [arrays], core_ids=[0])
    return tuple(r.results[0][f"out_{name}"] for name, _ in OUTPUTS)
```
